# Optimizing a Trainium2 kernel written in Bass

```python
import math
import jax, jax.numpy as jnp
from jax import lax
import numpy as np

D_MODEL = 1024
BATCH = 1
SEQ = 256
DEPTH = 2

HEAD_DIM = 64
FOX_HEADS = 8
SB_HEADS = 8
DIFF_HEADS = 4
DIFF_VDIM = 2 * HEAD_DIM
FOX_WIDTH = FOX_HEADS * HEAD_DIM
SB_WIDTH = SB_HEADS * HEAD_DIM
DIFF_QK_WIDTH = DIFF_HEADS * 2 * HEAD_DIM
DIFF_V_WIDTH = DIFF_HEADS * DIFF_VDIM
BRANCH_WIDTH = 512
N_BRANCHES = 3
Q_BLOCK = 128
FFN_DIM = 3584
N_EXPERTS = 8
TOP_K = 2
RMS_EPS = 1e-6
ALIBI_MAX_BIAS = 8.0
N_DENSE = (DEPTH + 1) // 2
N_MOE = DEPTH // 2
SPLIT_SIZES = (FOX_WIDTH, FOX_WIDTH, FOX_WIDTH, FOX_HEADS,
               SB_WIDTH, SB_WIDTH, SB_WIDTH,
               DIFF_QK_WIDTH, DIFF_QK_WIDTH, DIFF_V_WIDTH,
               N_BRANCHES * D_MODEL)
IN_DIM = sum(SPLIT_SIZES)

kernel_name = 'hybrid_fox_stickbreak_diffattn_moe_block'

def rmsnorm(x, g):
    xf = x.astype(jnp.float32)
    ms = jnp.mean(xf * xf, axis=-1, keepdims=True)
    return (xf * lax.rsqrt(ms + RMS_EPS) * g.astype(jnp.float32)).astype(x.dtype)

def to_heads(t, n_heads):
    b, s, _ = t.shape
    return t.reshape(b, s, n_heads, -1).transpose(0, 2, 1, 3)

def from_heads(t):
    b, h, s, d = t.shape
    return t.transpose(0, 2, 1, 3).reshape(b, s, h * d)

def block_positions(t0, t1):
    t_idx = t0 + jnp.arange(t1 - t0)[:, None]
    s_idx = jnp.arange(t1)[None, :]
    return t_idx, s_idx

def fox_attention(q, k, v, log_f):
    seq = q.shape[2]
    cum_f = jnp.cumsum(log_f, axis=-1)
    scale = HEAD_DIM ** -0.5
    outs = []
    for blk in range(seq // Q_BLOCK):
        t0, t1 = blk * Q_BLOCK, (blk + 1) * Q_BLOCK
        t_idx, s_idx = block_positions(t0, t1)
        logits = jnp.einsum('bhtd,bhsd->bhts', q[:, :, t0:t1], k[:, :, :t1]).astype(jnp.float32) * scale
        logits = logits + cum_f[:, :, t0:t1, None] - cum_f[:, :, None, :t1]
        logits = jnp.where(s_idx <= t_idx, logits, -jnp.inf)
        p = jax.nn.softmax(logits, axis=-1)
        outs.append(jnp.einsum('bhts,bhsd->bhtd', p.astype(v.dtype), v[:, :, :t1]))
    return jnp.concatenate(outs, axis=2)

def stick_breaking_attention(q, k, v):
    seq = q.shape[2]
    scale = HEAD_DIM ** -0.5
    outs = []
    for blk in range(seq // Q_BLOCK):
        t0, t1 = blk * Q_BLOCK, (blk + 1) * Q_BLOCK
        t_idx, s_idx = block_positions(t0, t1)
        z = jnp.einsum('bhtd,bhsd->bhts', q[:, :, t0:t1], k[:, :, :t1]).astype(jnp.float32) * scale
        mask = s_idx < t_idx
        log_stay = jnp.where(mask, jax.nn.log_sigmoid(-z), 0.0)
        tail = lax.cumsum(log_stay, axis=3, reverse=True) - log_stay
        log_a = jax.nn.log_sigmoid(z) + tail
        a = jnp.where(mask, jnp.exp(log_a), 0.0)
        outs.append(jnp.einsum('bhts,bhsd->bhtd', a.astype(v.dtype), v[:, :, :t1]))
    return jnp.concatenate(outs, axis=2)

def alibi_slopes(n_heads):
    h = jnp.arange(1, n_heads + 1, dtype=jnp.float32)
    return jnp.exp2(-ALIBI_MAX_BIAS * h / n_heads)

def diff_attention(q, k, v, lam):
    seq = q.shape[2]
    scale = HEAD_DIM ** -0.5
    q1, q2 = q[..., :HEAD_DIM], q[..., HEAD_DIM:]
    k1, k2 = k[..., :HEAD_DIM], k[..., HEAD_DIM:]
    slopes = alibi_slopes(q.shape[1])[:, None, None]
    outs = []
    for blk in range(seq // Q_BLOCK):
        t0, t1 = blk * Q_BLOCK, (blk + 1) * Q_BLOCK
        t_idx, s_idx = block_positions(t0, t1)
        mask = s_idx <= t_idx
        bias = -slopes * (t_idx - s_idx).astype(jnp.float32)
        l1 = jnp.einsum('bhtd,bhsd->bhts', q1[:, :, t0:t1], k1[:, :, :t1]).astype(jnp.float32) * scale + bias
        l2 = jnp.einsum('bhtd,bhsd->bhts', q2[:, :, t0:t1], k2[:, :, :t1]).astype(jnp.float32) * scale + bias
        p1 = jax.nn.softmax(jnp.where(mask, l1, -jnp.inf), axis=-1)
        p2 = jax.nn.softmax(jnp.where(mask, l2, -jnp.inf), axis=-1)
        p = p1 - lam * p2
        outs.append(jnp.einsum('bhts,bhsd->bhtd', p.astype(v.dtype), v[:, :, :t1]))
    return jnp.concatenate(outs, axis=2)

def hybrid_mixer(h, w_in, fox_f_bias, diff_lambda, diff_subln_g, w_branch, w_out, lam_init):
    proj = h @ w_in
    offsets = np.cumsum(SPLIT_SIZES)[:-1].tolist()
    fq, fk, fv, ff, sq, sk, sv, dq, dk, dv, gl = jnp.split(proj, offsets, axis=-1)
    log_f = jax.nn.log_sigmoid(ff.astype(jnp.float32) + fox_f_bias.astype(jnp.float32)).transpose(0, 2, 1)
    o_fox = from_heads(fox_attention(to_heads(fq, FOX_HEADS), to_heads(fk, FOX_HEADS),
                                     to_heads(fv, FOX_HEADS), log_f))
    o_sb = from_heads(stick_breaking_attention(to_heads(sq, SB_HEADS), to_heads(sk, SB_HEADS),
                                               to_heads(sv, SB_HEADS)))
    dl = diff_lambda.astype(jnp.float32)
    lam = jnp.exp(jnp.sum(dl[0] * dl[1])) - jnp.exp(jnp.sum(dl[2] * dl[3])) + lam_init
    o_d = diff_attention(to_heads(dq, DIFF_HEADS), to_heads(dk, DIFF_HEADS), to_heads(dv, DIFF_HEADS), lam)
    o_diff = from_heads(rmsnorm(o_d, diff_subln_g) * (1.0 - lam_init))
    branches = jnp.stack([o_fox, o_sb, o_diff], axis=2)
    projected = jnp.einsum('bsnc,ncd->bsnd', branches, w_branch)
    gates = jax.nn.sigmoid(gl.reshape(gl.shape[0], gl.shape[1], N_BRANCHES, D_MODEL))
    merged = jnp.sum(gates * projected, axis=2)
    return merged @ w_out

def swiglu(h, w_gate, w_up, w_down):
    return (jax.nn.silu(h @ w_gate) * (h @ w_up)) @ w_down

def moe_swiglu(h, router, w_gate, w_up, w_down):
    logits = (h @ router).astype(jnp.float32)
    top_vals, top_idx = lax.top_k(logits, TOP_K)
    weights = jax.nn.softmax(top_vals, axis=-1)
    combine = jnp.sum(jax.nn.one_hot(top_idx, N_EXPERTS, dtype=jnp.float32) * weights[..., None], axis=-2)
    out = jnp.zeros_like(h)
    for e in range(N_EXPERTS):
        out = out + combine[..., e:e + 1].astype(h.dtype) * swiglu(h, w_gate[e], w_up[e], w_down[e])
    return out

def ada_modulation(c, w, b):
    mod = jax.nn.silu(c) @ w + b
    shift, scale, gate = jnp.split(mod, 3, axis=-1)
    return shift[:, None, :], scale[:, None, :], gate[:, None, :]

def setup_inputs(seed: int = 0) -> dict:
    key = jax.random.key(seed)
    ks = jax.random.split(key, 20)
    f32 = jnp.float32
    def nrm(k, shape, s):
        return jax.random.normal(k, shape, f32) * s
    return {
        'x': nrm(ks[0], (BATCH, SEQ, D_MODEL), 1.0),
        'c': nrm(ks[1], (BATCH, D_MODEL), 1.0),
        'w_ada': nrm(ks[2], (DEPTH, 2, D_MODEL, 3 * D_MODEL), D_MODEL ** -0.5),
        'b_ada': nrm(ks[3], (DEPTH, 2, 3 * D_MODEL), 0.01),
        'norm_g': 1.0 + nrm(ks[4], (DEPTH, 4, D_MODEL), 0.02),
        'w_in': nrm(ks[5], (DEPTH, D_MODEL, IN_DIM), D_MODEL ** -0.5),
        'fox_f_bias': 2.0 + nrm(ks[6], (DEPTH, FOX_HEADS), 0.5),
        'diff_lambda': nrm(ks[7], (DEPTH, 4, HEAD_DIM), 0.1),
        'diff_subln_g': 1.0 + nrm(ks[8], (DEPTH, DIFF_VDIM), 0.02),
        'w_branch': nrm(ks[9], (DEPTH, N_BRANCHES, BRANCH_WIDTH, D_MODEL), BRANCH_WIDTH ** -0.5),
        'w_out': nrm(ks[10], (DEPTH, D_MODEL, D_MODEL), D_MODEL ** -0.5),
        'ffn_w_gate': nrm(ks[11], (N_DENSE, D_MODEL, FFN_DIM), D_MODEL ** -0.5),
        'ffn_w_up': nrm(ks[12], (N_DENSE, D_MODEL, FFN_DIM), D_MODEL ** -0.5),
        'ffn_w_down': nrm(ks[13], (N_DENSE, FFN_DIM, D_MODEL), FFN_DIM ** -0.5),
        'moe_router': nrm(ks[14], (N_MOE, D_MODEL, N_EXPERTS), D_MODEL ** -0.5),
        'moe_w_gate': nrm(ks[15], (N_MOE, N_EXPERTS, D_MODEL, FFN_DIM), D_MODEL ** -0.5),
        'moe_w_up': nrm(ks[16], (N_MOE, N_EXPERTS, D_MODEL, FFN_DIM), D_MODEL ** -0.5),
        'moe_w_down': nrm(ks[17], (N_MOE, N_EXPERTS, FFN_DIM, D_MODEL), FFN_DIM ** -0.5),
    }

def reference(x, c, w_ada, b_ada, norm_g, w_in, fox_f_bias, diff_lambda, diff_subln_g,
              w_branch, w_out, ffn_w_gate, ffn_w_up, ffn_w_down,
              moe_router, moe_w_gate, moe_w_up, moe_w_down):
    for layer in range(DEPTH):
        lam_init = 0.8 - 0.6 * math.exp(-0.3 * layer)
        shift, scale, gate = ada_modulation(c, w_ada[layer, 0], b_ada[layer, 0])
        h = rmsnorm(x, norm_g[layer, 0]) * (1.0 + scale) + shift
        y = hybrid_mixer(h, w_in[layer], fox_f_bias[layer], diff_lambda[layer], diff_subln_g[layer],
                         w_branch[layer], w_out[layer], lam_init)
        x = x + gate * rmsnorm(y, norm_g[layer, 1])
        shift, scale, gate = ada_modulation(c, w_ada[layer, 1], b_ada[layer, 1])
        h = rmsnorm(x, norm_g[layer, 2]) * (1.0 + scale) + shift
        if layer % 2 == 0:
            i = layer // 2
            y = swiglu(h, ffn_w_gate[i], ffn_w_up[i], ffn_w_down[i])
        else:
            i = layer // 2
            y = moe_swiglu(h, moe_router[i], moe_w_gate[i], moe_w_up[i], moe_w_down[i])
        x = x + gate * rmsnorm(y, norm_g[layer, 3])
    return x


_drawn_inputs = setup_inputs


def setup_inputs(seed=0):
    import zlib

    import numpy as np

    out = dict(_drawn_inputs(seed))
    spreads = {}
    factors = {}
    for name, (base, spread) in spreads.items():
        noise = np.random.default_rng([zlib.crc32(name.encode()), seed]).standard_normal(out[name].shape)
        drawn = base * np.exp(spread * noise) if base else spread * noise
        out[name] = __import__('jax').numpy.asarray(drawn.astype(out[name].dtype))
    for name, factor in factors.items():
        out[name] = (out[name] * factor).astype(out[name].dtype)
    return out
```

```python
import math
from contextlib import ExitStack

import concourse.bass as bass
from concourse import mybir

F32 = mybir.dt.float32
F32R = mybir.dt.float32r
I32 = mybir.dt.int32
ACT = mybir.ActivationFunctionType
ALU = mybir.AluOpType
AX = mybir.AxisListType

P = 128
D = 1024
SEQ = 256
TILES = SEQ // P
KC = D // P
HEAD = 64
NE = 8
FFN = 3584
NB = 512
UC = 2
FB = FFN // NB
HALF = D // NB
FOX, SB, DIFF = range(3)
EPS = 1e-6
MASKED = -float(2 ** 100)
FAR = -1e38

RAW = 6
SPLIT = 4
AHEAD = SPLIT - 1
ADA = 2

MIX_UNITS = 80
STEP_UNITS = 12
PASS_UNITS = STEP_UNITS * FB
MAX_OVER = 3
COLS = 1 + NE + MAX_OVER + 1

W_OFF = {}
_at = 0
for _name, _w in (("q0", 512), ("k0", 512), ("v0", 512), ("ff", 8), ("q1", 512), ("k1", 512),
                  ("v1", 512), ("q2", 512), ("k2", 512), ("v2", 512), ("gl", 3 * D)):
    W_OFF[_name] = _at
    _at += _w

JOBS = [(kind, n, 0) for n in range(3) for kind in "qkv"]
for _n in range(3):
    for _c in range(HALF):
        JOBS += [("br", _n, _c), ("gl", _n, _c)]
JOBS += [("out", 0, 0), ("out", 0, 1)]
UNITS = []
for _j, (_kind, _n, _c) in enumerate(JOBS[:-2]):
    _k = 4 if _kind == "br" else KC
    UNITS += [(_j, c, c == 0, c + UC == _k) for c in range(0, _k, UC)]
for _lo in (0, 4):
    for _c in range(HALF):
        UNITS += [(len(JOBS) - 2 + _c, c, c == 0, c + UC == KC) for c in (_lo, _lo + UC)]
assert len(UNITS) == MIX_UNITS
JOB_END = {u[0]: i for i, u in enumerate(UNITS)}

HEADS = [(FOX, h) for h in range(8)] + [(SB, h) for h in range(8)] + [(DIFF, h) for h in range(4)]
SCORE_AT = [13, 14, 16, 17, 19, 20, 22, 23] + [26, 27, 29, 30, 32, 33, 35, 36] + [39, 42, 45, 48]


def mixer_events():
    ev = [(0, "ff"), (1, "logf"), (2, "lam"), (3, "cum"), (4, "cumT"), (4, "lam2")]
    for n in range(3):
        e = 12 * n
        ev += [(e + 3, "evac", 3 * n), (e + 7, "evac", 3 * n + 1), (e + 11, "evac", 3 * n + 2)]
        ev += [(e + 5, "qkT", n, 0, 0), (e + 6, "qkT", n, 0, 1), (e + 9, "qkT", n, 1, 0), (e + 10, "qkT", n, 1, 1)]
    for k, at in enumerate(SCORE_AT):
        late = HEADS[k][0] == DIFF
        ev += [(at, "scores", k), (at + 1, "exp", k), (at + 3 + late, "probsT", k), (at + 5 + late, "values", k)]
        if late:
            ev.append((at + 2, "combine", k))
    ev += [(29, "oT", 0, 0), (30, "oT", 0, 1), (44, "oT", 1, 0), (45, "oT", 1, 1)]
    ev += [(55, "diffnorm"), (56, "diffscale"), (58, "oT", 2, 0), (59, "oT", 2, 1)]
    for n in range(3):
        for c in range(HALF):
            ev.append((JOB_END[9 + 4 * n + 2 * c + 1], "merge", n, c))
    ev += [(69, "mergedT", 0), (75, "mergedT", 1)]
    order = {"evac": 0, "merge": 0, "values": 2, "probsT": 3, "oT": 4, "qkT": 5, "scores": 6}
    return sorted(ev, key=lambda x: (x[0], order.get(x[1], 1)))


EVENTS = mixer_events()
T_USES = [e[1:] for e in EVENTS if e[1] in ("ff", "cum", "cumT", "qkT", "probsT", "oT")]
T_AT = {key: i for i, key in enumerate(T_USES)}
NT = len(T_USES)
NH = len(HEADS)

ADA_MIX = {0: [(0, 2), (1, 0), (1, 1), (1, 2)], 1: [(2, 2), (3, 0), (3, 1), (3, 2)]}
MIX_PIECES = 4 * KC
FFN_PIECES = 2 * KC
PIECE_AT = [2 + 2 * i for i in range(MIX_PIECES)]
PIECE_LEAD = AHEAD + 2


def region(s, part):
    return part if part < 2 else 2 + s % 2


def build(nc, x, c, w_ada, b_ada, norm_g, w_in, fox_f_bias, diff_lambda, diff_subln_g, w_branch,
          w_out, ffn_w_gate, ffn_w_up, ffn_w_down, moe_router, moe_w_gate, moe_w_up, moe_w_down, out):
    lam_init = [0.8 - 0.6 * math.exp(-0.3 * layer) for layer in range(2)]
    ctx = ExitStack()
    with ctx:
        def sb(name, shape, dt=F32, into=ctx):
            return into.enter_context(nc.sbuf_tensor(name, shape, dt))

        def sem(name):
            return ctx.enter_context(nc.semaphore(name))

        xs = sb("xs", [P, TILES, D])
        h = sb("h", [P, TILES, D])
        hT_hi = sb("hT_hi", [P, KC, SEQ], F32R)
        hT_lo = sb("hT_lo", [P, KC, SEQ], F32R)
        raw = sb("raw", [P, RAW, UC, NB])
        w_hi = sb("w_hi", [P, SPLIT, UC, NB], F32R)
        w_lo = sb("w_lo", [P, SPLIT, UC, NB], F32R)
        ada_piece = sb("ada_piece", [P, ADA, D])
        ada_sum = sb("ada_sum", [P, 4, D])
        ada_bias = sb("ada_bias", [P, D])
        mod_scale = sb("mod_scale", [P, D])
        mod_shift = sb("mod_shift", [P, D])
        mod_gate = sb("mod_gate", [P, D])
        g_pre = sb("g_pre", [P, D])
        g_post = sb("g_post", [P, D])
        c_col = sb("c_col", [P, KC])
        c_silu = sb("c_silu", [P, KC])
        ident = sb("ident", [P, P])
        ident_r = sb("ident_r", [P, P], F32R)
        ones = sb("ones", [P, P])
        tri = sb("tri", [P, P])
        tri_strict = sb("tri_strict", [P, P])
        stat = sb("stat", [P, 16])
        zero_r = sb("zero_r", [P, NB], F32R)
        c_cur = sb("c_cur", [P, 1])
        eps_col = sb("eps_col", [P, 1])
        one_col = sb("one_col", [P, 1])

        mix = ExitStack()
        values_in = sb("values_in", [P, 2, TILES, NB], into=mix)
        qkT = sb("qkT", [P, 2, 2, 4, SEQ], into=mix)
        staged = sb("staged", [P, TILES, NB], into=mix)
        oT_hi = sb("oT_hi", [P, 4, SEQ], F32R, into=mix)
        oT_lo = sb("oT_lo", [P, 4, SEQ], F32R, into=mix)
        o_rows = sb("o_rows", [P, 2, TILES, NB], into=mix)
        probs = sb("probs", [P, 2, 3 * P], into=mix)
        probsT = sb("probsT", [P, 2, 3 * P], into=mix)
        soft = sb("soft", [P, 2, 3 * P], into=mix)
        stay = sb("stay", [P, 3 * P], into=mix)
        tail = sb("tail", [P, 3 * P], into=mix)
        dist_r = sb("dist_r", [P, 3 * P], F32R, into=mix)
        slope_r = sb("slope_r", [P, 4, P], F32R, into=mix)
        mask_r = sb("mask_r", [P, 2, P], F32R, into=mix)
        maskf = sb("maskf", [P, 2 * P], into=mix)
        distf = sb("distf", [P, 3 * P], into=mix)
        zeros = sb("zeros", [P, SEQ], into=mix)
        wff = sb("wff", [P, KC, 8], into=mix)
        wff_hi = sb("wff_hi", [P, KC, 8], F32R, into=mix)
        wff_lo = sb("wff_lo", [P, KC, 8], F32R, into=mix)
        f_bias = sb("f_bias", [P, 8], into=mix)
        fgate = sb("fgate", [P, 4, TILES, 8], into=mix)
        cum = sb("cum", [P, TILES, P], into=mix)
        cumT = sb("cumT", [P, SEQ], into=mix)
        cum_mov = sb("cum_mov", [P, SEQ], into=mix)
        cum_sta = sb("cum_sta", [P, 2, SEQ], into=mix)
        pick = sb("pick", [P, 2], into=mix)
        dl = sb("dl", [P, 4, HEAD], into=mix)
        lam = sb("lam", [P, 8], into=mix)
        subln = sb("subln", [P, P], into=mix)
        hstat = sb("hstat", [P, 4, 12], into=mix)
        dstat = sb("dstat", [P, 2, 8], into=mix)
        mix.close()
        start_stack = ExitStack()
        ada_start = sb("ada_start", [P, KC, 2, D], into=start_stack)
        start_stack.close()
        ffn_stack = ExitStack()
        aT_hi = sb("aT_hi", [P, 4, SEQ], F32R, into=ffn_stack)
        aT_lo = sb("aT_lo", [P, 4, SEQ], F32R, into=ffn_stack)
        gate_s = sb("gate_s", [P, TILES, NB], into=ffn_stack)
        act_s = sb("act_s", [P, TILES, NB], into=ffn_stack)
        xg_hi = sb("xg_hi", [P, KC, P], F32R, into=ffn_stack)
        xg_lo = sb("xg_lo", [P, KC, P], F32R, into=ffn_stack)
        y_acc = sb("y_acc", [P, TILES, D], into=ffn_stack)
        y_exp = sb("y_exp", [P, D], into=ffn_stack)
        pick_rows = sb("pick_rows", [P, TILES, P], into=ffn_stack)
        pick_cols = sb("pick_cols", [P, SEQ], into=ffn_stack)
        slots = sb("slots", [P, P], into=ffn_stack)
        wr = sb("wr", [P, KC, NE], into=ffn_stack)
        wr_hi = sb("wr_hi", [P, KC, NE], F32R, into=ffn_stack)
        wr_lo = sb("wr_lo", [P, KC, NE], F32R, into=ffn_stack)
        rt = sb("rt", [P, 20, TILES, NE], into=ffn_stack)
        route = sb("route", [P, 3, TILES, NE], into=ffn_stack)
        rank = sb("rank", [P, TILES, NE], into=ffn_stack)
        index = sb("index", [P, NE], into=ffn_stack)
        rs = sb("rs", [P, 16, TILES], into=ffn_stack)
        table = sb("table", [P, COLS, 3, TILES], into=ffn_stack)
        cur = sb("cur", [P, 3, TILES], into=ffn_stack)
        cur_w = sb("cur_w", [P, TILES], into=ffn_stack)
        expert_f = sb("expert_f", [P, 16], into=ffn_stack)
        expert_i = sb("expert_i", [P, 16], I32, into=ffn_stack)
        ffn_stack.close()

        ps = ctx.enter_context(nc.psum_tensor("ps", [P, 8, NB], F32))
        psT = ps[:, 6]
        psO = ps[:, 7]

        raw_landed = [sem(f"raw_landed{i}") for i in range(RAW)]
        hi_ready, lo_ready, unit_used = sem("hi_ready"), sem("lo_ready"), sem("unit_used")
        ada_landed = [sem(f"ada_landed{i}") for i in range(ADA)]
        ada_used, bias_landed, bias_used = sem("ada_used"), sem("bias_landed"), sem("bias_used")
        start_landed = [sem(f"start_landed{i}") for i in range(KC)]
        start_used, x_landed, c_landed = sem("start_used"), sem("x_landed"), sem("c_landed")
        small_landed, gpre_landed, gpost_landed = sem("small_landed"), sem("gpre_landed"), sem("gpost_landed")
        router_landed, consts_ready, mixconst_ready = sem("router_landed"), sem("consts_ready"), sem("mixconst_ready")
        mask_ready, c_ready = sem("mask_ready"), sem("c_ready")
        sums_bcast, gate_ready, shift_ready, scale_ready = (
            sem("sums_bcast"), sem("gate_ready"), sem("shift_ready"), sem("scale_ready"))
        rstd_ready, x_ready, h_ready = sem("rstd_ready"), sem("x_ready"), sem("h_ready")
        hT_filled, hT_half, hT_ready = sem("hT_filled"), sem("hT_half"), sem("hT_ready")
        job_read, merged_ready = sem("job_read"), sem("merged_ready")
        wff_half, wff_ready = sem("wff_half"), sem("wff_ready")
        fpre_ready, fsoft_ready, logf_ready = sem("fpre_ready"), sem("fsoft_ready"), sem("logf_ready")
        cumrows_ready, cummov_ready, cumsta_ready = sem("cumrows_ready"), sem("cummov_ready"), sem("cumsta_ready")
        scores_done, max_ready, exp_done, comb_done = (
            sem("scores_done"), sem("max_ready"), sem("exp_done"), sem("comb_done"))
        soft_ready, loga_ready = sem("soft_ready"), sem("loga_ready")
        t_filled, t_half, t_read = sem("t_filled"), sem("t_half"), sem("t_read")
        values_done, o_ready = sem("values_done"), sem("o_ready")
        mT_filled, mT_half, mT_ready = sem("mT_filled"), sem("mT_half"), sem("mT_ready")
        lam_a, lam_b = sem("lam_a"), sem("lam_b")
        dsum_ready, drstd_ready, dscaled = sem("dsum_ready"), sem("drstd_ready"), sem("dscaled")
        silu_done, act_done, ccur_ready, idr_ready = sem("silu_done"), sem("act_done"), sem("ccur_ready"), sem("idr_ready")
        aT_filled, aT_half, aT_ready = sem("aT_filled"), sem("aT_half"), sem("aT_ready")
        yexp_zero, yexp_copied = sem("yexp_zero"), sem("yexp_copied")
        wr_half, wr_ready = sem("wr_half"), sem("wr_ready")
        router_done, wdiff_ready, wexp_ready, sel_ready = (
            sem("router_done"), sem("wdiff_ready"), sem("wexp_ready"), sem("sel_ready"))
        count_done, passes_ready, moeconst_ready = sem("count_done"), sem("passes_ready"), sem("moeconst_ready")
        rows_picked, cols_filled, cols_ready = sem("rows_picked"), sem("cols_filled"), sem("cols_ready")
        gathered, xg_half, xg_ready = sem("gathered"), sem("xg_half"), sem("xg_ready")
        scattered, summed, cur_ready, curw_ready = sem("scattered"), sem("summed"), sem("cur_ready"), sem("curw_ready")
        act_own, dve_own, pool_own, stored = sem("act_own"), sem("dve_own"), sem("pool_own"), sem("stored")

        class Own:

            def __init__(self, eng, s):
                self.eng, self.s, self.n = eng, s, 0

            def __call__(self, ins):
                self.n += 1
                ins.then_inc(self.s, 1)
                self.eng.wait_ge(self.s, self.n)

        MIX_AT = [0, MIX_UNITS + PASS_UNITS]
        FFN_AT = [MIX_UNITS, 2 * MIX_UNITS + PASS_UNITS]
        PIECE0 = [0, MIX_PIECES, MIX_PIECES + FFN_PIECES]
        BIAS0 = [2, 6, 8]
        PIECES_BY_END = [MIX_PIECES, MIX_PIECES + FFN_PIECES, 2 * MIX_PIECES + FFN_PIECES,
                         2 * MIX_PIECES + FFN_PIECES]

        def place(u):
            const, step, pas = u
            return step * STEP_UNITS + pas * PASS_UNITS + const

        def landings(u):
            const, step, pas = u
            return step * (16 * STEP_UNITS // RAW) + pas * (16 * PASS_UNITS // RAW) + 16 * (const // RAW + 1)

        def chunks(w):
            return w.rearrange("(c p) n -> p c n", p=P)

        def unit_source(layer, i):
            j, c0, _, _ = UNITS[i]
            kind, n, col = JOBS[j]
            if kind == "br":
                w, at = w_branch[layer, n], NB * col
            elif kind == "out":
                w, at = w_out[layer], NB * col
            elif kind == "gl":
                w, at = w_in[layer], W_OFF["gl"] + n * D + NB * col
            else:
                w, at = w_in[layer], W_OFF[f"{kind}{n}"]
            return chunks(w)[:, c0:c0 + UC, at:at + NB]

        def pair(j):
            return (j % 2) * 2 if j < len(JOBS) - 2 else 2 * JOBS[j][2]

        def half_rows(tile, n0=0):
            return tile.rearrange("p (a n) -> p a n", a=HALF)

        def y_banks(t):
            return ps[:, 0:4, :].rearrange("p (c t) n -> p t c n", t=TILES)[:, t]

        def by_chunk(tile):
            return tile.rearrange("p (a c) k -> p a (c k)", a=HALF)

        def by_tile(hT, c0=0, nc_=KC):
            return hT[:, c0:c0 + nc_, :].rearrange("p c (t k) -> p t c k", t=TILES)

        def ada_rows(s):
            return w_ada[s // 2, s % 2].rearrange("(p k) n -> k p n", k=KC)

        def rows_of_g(layer, k):
            return norm_g[layer, k:k + 1, :].partition_broadcast(P)

        def job_reads(layer, j):
            return 15 * layer + (j + 1 if j < 9 else 9 + (j - 8) // 2)

        def merges(layer, j):
            return 6 * layer + (j - 9) // 2 + 1

        block = ctx.enter_context(nc.Block())

        @block.sync
        def _(sp):
            def load_unit(u, src):
                if not (isinstance(u[1], int) and isinstance(u[2], int) and place(u) < RAW):
                    sp.wait_ge(lo_ready, place(u) - RAW + 1)
                sp.dma_start(raw[:, u[0] % RAW], src).then_inc(raw_landed[u[0] % RAW], 16)

            def load_piece(p, s, part, c0):
                if not (isinstance(p[1], int) and p[0] + p[1] < ADA):
                    sp.wait_ge(ada_used, p[1] + (p[0] - ADA + 1))
                w = ada_rows(s)
                row = w[c0] if isinstance(c0, int) else w[bass.ds(c0, 1)].rearrange("o p n -> p (o n)")
                sp.dma_start(ada_piece[:, p[0] % ADA], row[:, part * D:(part + 1) * D]
                             ).then_inc(ada_landed[p[0] % ADA], 16)

            def load_bias(k, s, part):
                if k:
                    sp.wait_ge(bias_used, k)
                sp.dma_start(ada_bias[0:1, :], b_ada[s // 2, s % 2:s % 2 + 1, part * D:(part + 1) * D]
                             ).then_inc(bias_landed, 16)

            def load_g(s):
                sp.wait_ge(scale_ready, s + 1)
                if s < 3:
                    sp.dma_start(g_pre[:], rows_of_g((s + 1) // 2, 2 * ((s + 1) % 2))).then_inc(gpre_landed, 16)
                if s:
                    sp.wait_ge(gate_ready, s)
                sp.dma_start(g_post[:], rows_of_g(s // 2, 2 * (s % 2) + 1)).then_inc(gpost_landed, 16)

            def mixer(layer):
                p = 0
                for i in range(MIX_UNITS):
                    if i == RAW:
                        if layer:
                            sp.wait_ge(unit_used, MIX_AT[1])
                        else:
                            sp.wait_ge(start_used, 2 * KC)
                        sp.dma_start(wff[:], chunks(w_in[layer])[:, :, W_OFF["ff"]:W_OFF["ff"] + 8]
                                     ).then_inc(small_landed, 16)
                        sp.dma_start(f_bias[:], fox_f_bias[layer:layer + 1, :].partition_broadcast(P)
                                     ).then_inc(small_landed, 16)
                        sp.dma_start(dl[:], diff_lambda[layer:layer + 1].partition_broadcast(P)
                                     ).then_inc(small_landed, 16)
                        sp.dma_start(subln[:], diff_subln_g[layer:layer + 1, :].partition_broadcast(P)
                                     ).then_inc(small_landed, 16)
                    if i == RAW + 4:
                        load_g(2 * layer)
                    while p < MIX_PIECES and PIECE_AT[p] + PIECE_LEAD <= i:
                        s, part = ADA_MIX[layer][p // KC]
                        if p % KC == 0:
                            load_bias(BIAS0[2 * layer] + p // KC, s, part)
                        load_piece((PIECE0[2 * layer] + p, 0), s, part, p % KC)
                        p += 1
                    load_unit((MIX_AT[layer] + i, 0, 0), unit_source(layer, i))

            def ffn(u0, pas, w_gate, w_up, w_down, dense):
                def wide(at, step, w, cols):
                    for k in range(4):
                        load_unit((u0 + at + k, step, pas), chunks(w)[:, UC * k:UC * (k + 1), cols])

                def down(at, step, f):
                    rows = w_down.rearrange("(f r) n -> f r n", r=NB)
                    rows = rows[f] if isinstance(f, int) else rows[bass.ds(f, 1)].rearrange("o r n -> (o r) n")
                    for k in range(4):
                        load_unit((u0 + at + k, step, pas), chunks(rows)[
                            :, UC * (k % 2):UC * (k % 2 + 1), NB * (k // 2):NB * (k // 2 + 1)])

                wide(0, 0, w_gate, slice(0, NB))
                wide(4, 0, w_up, slice(0, NB))
                if dense:
                    load_g(1)
                    for part in range(2):
                        load_bias(BIAS0[1] + part, 2, part)
                        load_piece((PIECE0[1] + part, 0), 2, part, 0)
                with sp.Fori(1, FB) as f:
                    wide(8, f - 1, w_gate, bass.ds(f * NB, NB))
                    if dense:
                        for part in range(2):
                            load_piece((PIECE0[1] + 2 + part, (f - 1) * 2), 2, part, f)
                    wide(12, f - 1, w_up, bass.ds(f * NB, NB))
                    down(16, f - 1, f - 1)
                if dense:
                    for part in range(2):
                        load_piece((PIECE0[1] + 14 + part, 0), 2, part, KC - 1)
                down(PASS_UNITS - 4, 0, FB - 1)

            def expert(w, e):
                return w[0].rearrange("e k n -> e k n")[bass.ds(e, 1)].rearrange("o k n -> (o k) n")

            sp.dma_start(c_col[:], c.rearrange("b (p k) -> p (b k)", p=P)).then_inc(c_landed, 16)
            for k in range(KC):
                sp.dma_start(ada_start[:, k], ada_rows(0)[k][:, 0:2 * D].rearrange(
                    "p (a n) -> p a n", a=2)).then_inc(start_landed[k], 16)
                if k < 2:
                    if k == 0:
                        sp.wait_ge(consts_ready, 1)
                    load_bias(k, 0, k)
            sp.dma_start(xs[:], x.rearrange("b (t p) d -> p (b t) d", p=P)).then_inc(x_landed, 16)
            sp.dma_start(g_pre[:], rows_of_g(0, 0)).then_inc(gpre_landed, 16)
            mixer(0)
            ffn(FFN_AT[0], 0, ffn_w_gate[0], ffn_w_up[0], ffn_w_down[0], True)
            mixer(1)
            sp.wait_ge(unit_used, FFN_AT[1])
            sp.dma_start(wr[:], chunks(moe_router[0])).then_inc(router_landed, 16)
            sp.wait_ge(gate_ready, 3)
            sp.dma_start(g_post[:], rows_of_g(1, 3)).then_inc(gpost_landed, 16)
            with sp.Fori(0, NE) as e:
                ffn(FFN_AT[1], e, expert(moe_w_gate, e), expert(moe_w_up, e), expert(moe_w_down, e), False)
            sp.wait_ge(passes_ready, 1)
            passes = sp.value_load(expert_i[0:1, MAX_OVER:MAX_OVER + 1], min_val=NE, max_val=NE + MAX_OVER)
            for j in range(MAX_OVER):
                with sp.If(passes > NE + j):
                    again = sp.value_load(expert_i[0:1, j:j + 1], min_val=0, max_val=NE - 1)
                    ffn(FFN_AT[1], NE + j, expert(moe_w_gate, again), expert(moe_w_up, again),
                        expert(moe_w_down, again), False)
            for t in range(TILES):
                sp.wait_ge(x_ready, 7 + t)
                sp.dma_start(out[0, t * P:(t + 1) * P, :], xs[:, t]).then_inc(stored, 16)
            sp.wait_ge(stored, 16 * TILES)

        @block.gpsimd
        def _(pool):
            own = Own(pool, pool_own)
            own(nc.gpsimd.memset(ada_bias[:], 0.0))
            own(nc.gpsimd.memset(ones[:], 1.0))
            own(nc.gpsimd.memset(eps_col[:], EPS))
            own(nc.gpsimd.memset(one_col[:], 1.0))
            own(nc.gpsimd.memset(ident[:], 0.0))
            own(nc.gpsimd.affine_select(out=ident[:], in_=ident[:], compare_op=ALU.not_equal, fill=1.0,
                                        base=0, pattern=[[-1, P]], channel_multiplier=1))
            own(nc.gpsimd.affine_select(out=tri[:], in_=ones[:], compare_op=ALU.is_ge, fill=0.0,
                                        base=0, pattern=[[1, P]], channel_multiplier=-1))
            nc.gpsimd.affine_select(out=tri_strict[:], in_=ones[:], compare_op=ALU.is_gt, fill=0.0,
                                    base=0, pattern=[[1, P]], channel_multiplier=-1).then_inc(consts_ready, 1)

            for layer in range(2):
                if layer:
                    pool.wait_ge(unit_used, MIX_AT[1])
                else:
                    pool.wait_ge(start_used, 2 * KC)
                own(nc.gpsimd.memset(zeros[:], 0.0))
                own(nc.gpsimd.memset(cum[:], 0.0))
                own(nc.gpsimd.memset(pick[:], 1.0))
                own(nc.gpsimd.affine_select(out=pick[:, 0:1], in_=pick[:, 0:1], compare_op=ALU.is_ge, fill=0.0,
                                            base=7, pattern=[[0, 1]], channel_multiplier=-1))
                own(nc.gpsimd.affine_select(out=pick[:, 1:2], in_=pick[:, 1:2], compare_op=ALU.is_ge, fill=0.0,
                                            base=-8, pattern=[[0, 1]], channel_multiplier=1))
                own(nc.gpsimd.affine_select(out=pick[:, 1:2], in_=pick[:, 1:2], compare_op=ALU.is_ge, fill=0.0,
                                            base=15, pattern=[[0, 1]], channel_multiplier=-1))
                for m, op in enumerate((ALU.is_ge, ALU.is_gt)):
                    own(nc.gpsimd.affine_select(out=maskf[:, m * P:(m + 1) * P], in_=zeros[:, 0:P], compare_op=op,
                                                fill=MASKED, base=0, pattern=[[-1, P]], channel_multiplier=1))
                for b in range(TILES):
                    at = distf[:, b * P:(2 * b + 1) * P]
                    own(nc.gpsimd.iota(at, pattern=[[1, (b + 1) * P]], base=-b * P, channel_multiplier=-1,
                                       allow_small_or_imprecise_dtypes=True))
                    own(nc.gpsimd.affine_select(out=at, in_=at, compare_op=ALU.is_ge, fill=MASKED, base=b * P,
                                                pattern=[[-1, (b + 1) * P]], channel_multiplier=1))
                nc.gpsimd.memset(lam[:], 0.0).then_inc(mixconst_ready, 1)
                pool.wait_ge(t_read, NT * layer + T_AT[("cumT",)] + 1)
                own(nc.gpsimd.tensor_scalar(cum_mov[:], cumT[:], pick[:, 1:2], pick[:, 0:1], ALU.mult, ALU.add))
                for k in range(8):
                    if k >= 2:
                        pool.wait_ge(scores_done, NH * layer + k - 1)
                    nc.gpsimd.tensor_scalar(cum_sta[:, k % 2], cumT[:], ident[:, k:k + 1], ident[:, 8 + k:9 + k],
                                            ALU.mult, ALU.add).then_inc(cumsta_ready, 1)

            pool.wait_ge(unit_used, FFN_AT[1])
            own(nc.gpsimd.memset(table[:], 0.0))
            own(nc.gpsimd.memset(y_acc[:], 0.0))
            own(nc.gpsimd.memset(route[:], 0.0))
            own(nc.gpsimd.iota(slots[:], pattern=[[1, P]], base=0, channel_multiplier=0,
                               allow_small_or_imprecise_dtypes=True))
            own(nc.gpsimd.iota(rank[:], pattern=[[0, TILES], [-1, NE]], base=NE, channel_multiplier=0,
                               allow_small_or_imprecise_dtypes=True))
            nc.gpsimd.iota(index[:], pattern=[[1, NE]], base=0, channel_multiplier=0,
                           allow_small_or_imprecise_dtypes=True).then_inc(moeconst_ready, 1)

        @block.tensor
        def _(pe):
            mm = nc.tensor.matmul

            def unit(u, banks, stationary, c0, opens, closes):
                s = u[0] % SPLIT
                pe.wait_ge(lo_ready, place(u) + 1)
                for t, bank in enumerate(banks):
                    for k in range(UC):
                        hi, lo = stationary(t, c0 + k)
                        mm(bank, hi, w_hi[:, s, k], start=opens and k == 0, stop=False)
                        mm(bank, hi, w_lo[:, s, k], start=False, stop=False)
                        last = mm(bank, lo, w_hi[:, s, k], start=False, stop=closes and k == UC - 1)
                return last.then_inc(unit_used, 1)

            def of(hi, lo):
                return lambda t, c: (hi[:, c, t * P:(t + 1) * P], lo[:, c, t * P:(t + 1) * P])

            def bcast_sum(r, bank):
                for c in range(HALF):
                    last = mm(ps[:, bank + c], ones[:], ada_sum[:, r, c * NB:(c + 1) * NB], start=True, stop=True)
                last.then_inc(sums_bcast, 1)

            def close(s):
                pe.wait_ge(ada_used, PIECES_BY_END[s])
                if s in (0, 2):
                    pe.wait_ge(mT_ready, s + 2)
                elif s == 1:
                    pe.wait_ge(aT_ready, FB)
                bcast_sum(region(s, 2), 6)

            def norm(s):
                if s == 0:
                    pe.wait_ge(consts_ready, 1)
                    pe.wait_ge(start_used, 2 * KC)
                bcast_sum(0, 4)
                if s:
                    pe.wait_ge(gate_ready, s)
                bcast_sum(1, 6)
                for t in range(TILES):
                    if t == 0:
                        pe.wait_ge(shift_ready, s + 1)
                    else:
                        pe.wait_ge(scale_ready, s + 1)
                    pe.wait_ge(h_ready, 2 * s + t + 1)
                    for k in range(KC):
                        last = nc.tensor.transpose(ps[:, 4 + 2 * t + k // 4, (k % 4) * P:(k % 4 + 1) * P],
                                                   h[:, t, k * P:(k + 1) * P], ident[:])
                    last.then_inc(hT_filled, 1)
                pe.wait_ge(hT_ready, 2 * s + 2)

            def mixer(layer):
                heads0, uses0 = NH * layer, NT * layer

                def take_t(key):
                    if uses0 + T_AT[key]:
                        pe.wait_ge(t_read, uses0 + T_AT[key])

                def event(e):
                    what, key = e[1], e[1:]
                    if what == "ff":
                        take_t(key)
                        pe.wait_ge(wff_ready, layer + 1)
                        for t in range(TILES):
                            for k in range(KC):
                                hi, lo = of(hT_hi, hT_lo)(t, k)
                                o = psT[:, 8 * t:8 * t + 8]
                                mm(o, hi, wff_hi[:, k], start=k == 0, stop=False)
                                mm(o, hi, wff_lo[:, k], start=False, stop=False)
                                last = mm(o, lo, wff_hi[:, k], start=False, stop=k == KC - 1)
                        last.then_inc(t_filled, 1)
                    elif what == "cum":
                        take_t(key)
                        pe.wait_ge(logf_ready, layer + 1)
                        mm(psT[:, 0:8], tri[:], fgate[:, 3, 0], start=True, stop=True)
                        mm(psT[:, 8:16], ones[:], fgate[:, 3, 0], start=True, stop=False)
                        mm(psT[:, 8:16], tri[:], fgate[:, 3, 1], start=False, stop=True).then_inc(t_filled, 1)
                    elif what == "cumT":
                        take_t(key)
                        pe.wait_ge(cumrows_ready, layer + 1)
                        for t in range(TILES):
                            last = nc.tensor.transpose(psT[:, t * P:(t + 1) * P], cum[:, t], ident[:])
                        last.then_inc(t_filled, 1)
                    elif what == "qkT":
                        _, _, n, qk, t = e
                        take_t(key)
                        pe.wait_ge(job_read, job_reads(layer, 3 * n + qk))
                        for k in range(4):
                            last = nc.tensor.transpose(psT[:, k * P:(k + 1) * P], staged[:, t, k * P:(k + 1) * P],
                                                       ident[:])
                        last.then_inc(t_filled, 1)
                    elif what == "scores":
                        scores(e[2])
                    elif what == "probsT":
                        k = e[2]
                        take_t(key)
                        if HEADS[k][0] == DIFF:
                            pe.wait_ge(comb_done, 4 * layer + k - 15)
                        else:
                            pe.wait_ge(exp_done, heads0 + k + 1)
                        buf = 0 if HEADS[k][0] == DIFF else k % 2
                        for b in range(3):
                            last = nc.tensor.transpose(psT[:, b * P:(b + 1) * P], probs[:, buf, b * P:(b + 1) * P],
                                                       ident[:])
                        last.then_inc(t_filled, 1)
                    elif what == "values":
                        values(e[2])
                    elif what == "oT":
                        _, _, n, t = e
                        take_t(key)
                        if n == DIFF:
                            pe.wait_ge(dscaled, layer + 1)
                        else:
                            pe.wait_ge(o_ready, heads0 + 8 * (n + 1))
                        for k in range(4):
                            last = nc.tensor.transpose(psT[:, k * P:(k + 1) * P],
                                                       o_rows[:, n % 2, t, k * P:(k + 1) * P], ident[:])
                        last.then_inc(t_filled, 1)
                    elif what == "mergedT":
                        half = e[2]
                        pe.wait_ge(merged_ready, 6 * layer + 5 + half)
                        if half == 0:
                            pe.wait_ge(exp_done, heads0 + NH)
                        else:
                            pe.wait_ge(t_read, uses0 + NT)
                            pe.wait_ge(o_ready, heads0 + NH)
                        for t in range(TILES):
                            for k in range(4):
                                last = nc.tensor.transpose(
                                    ps[:, 4 + 2 * half + t, k * P:(k + 1) * P],
                                    h[:, t, half * NB + k * P:half * NB + (k + 1) * P], ident[:])
                        last.then_inc(mT_filled, 1)

                def scores(k):
                    branch, hd = HEADS[k]
                    n = branch % 2
                    maps = 2 if branch == DIFF else 1
                    if k >= 2:
                        last_user = k - 1 if branch == DIFF else k - 2
                        if HEADS[last_user][0] == SB:
                            pe.wait_ge(loga_ready, 8 * layer + last_user - 7)
                        else:
                            pe.wait_ge(exp_done, heads0 + last_user + 1)
                    if k in (0, 8, 16):
                        pe.wait_ge(t_read, uses0 + T_AT[("qkT", branch, 1, 1)] + 1)
                    if branch == FOX:
                        pe.wait_ge(cumsta_ready, 8 * layer + k + 1)
                        pe.wait_ge(mask_ready, layer + 1)
                    for m in range(maps):
                        bank = ps[:, 4 + (m if branch == DIFF else k % 2)]
                        for b in range(TILES):
                            keys = (b + 1) * P
                            o = bank[:, b * P:b * P + keys]
                            diag = bank[:, 2 * b * P:(2 * b + 1) * P]
                            if branch == FOX:
                                mm(o, cum_sta[:, k % 2, b * P:(b + 1) * P], cum_mov[:, 0:keys], start=True, stop=False,
                                   skip_group_check=True)
                                mm(diag, ident_r[:], mask_r[:, 0], start=False, stop=False, skip_group_check=True)
                            elif branch == SB:
                                mm(diag, ident_r[:], mask_r[:, 1], start=True, stop=False, skip_group_check=True)
                            else:
                                mm(o, slope_r[:, hd], dist_r[:, b * P:b * P + keys], start=True, stop=False,
                                   skip_group_check=True)
                            half = m if branch == DIFF else hd % 2
                            chunk = hd if branch == DIFF else hd // 2
                            rows = slice(half * HEAD, (half + 1) * HEAD)
                            last = mm(o, qkT[rows, n, 0, chunk, b * P:(b + 1) * P], qkT[rows, n, 1, chunk, 0:keys],
                                      start=False, stop=True, skip_group_check=True)
                    last.then_inc(scores_done, 1)

                def values(k):
                    branch, hd = HEADS[k]
                    n = branch % 2
                    pe.wait_ge(t_read, uses0 + T_AT[("probsT", k)] + 1)
                    if k:
                        pe.wait_ge(o_ready, heads0 + k)
                    if branch == FOX and k == 0:
                        pe.wait_ge(job_read, job_reads(layer, 2))
                    if branch == SB and k == 8:
                        pe.wait_ge(job_read, job_reads(layer, 5))
                    if branch == DIFF and k == 16:
                        pe.wait_ge(job_read, job_reads(layer, 8))
                    width, at = (P, (k % 2) * 2 * P) if branch == DIFF else (HEAD, (k % 4) * P)
                    for b in range(TILES):
                        o = psO[:, at + b * width:at + (b + 1) * width]
                        for s in range(b + 1):
                            last = mm(o, probsT[:, k % 2, (b + s) * P:(b + s + 1) * P],
                                      values_in[:, n, s, hd * width:(hd + 1) * width], start=s == 0, stop=s == b)
                    last.then_inc(values_done, 1)

                ev = list(EVENTS)
                for i, (j, c0, opens, closes) in enumerate(UNITS):
                    kind, n, col = JOBS[j]
                    if opens:
                        before = {len(JOBS) - 2: j - 1, len(JOBS) - 1: j - 3}.get(j, j - 2)
                        if before >= 0:
                            if JOBS[before][0] == "br":
                                pe.wait_ge(merged_ready, merges(layer, before))
                            else:
                                pe.wait_ge(job_read, job_reads(layer, before))
                        if kind == "br":
                            pe.wait_ge(t_read, uses0 + T_AT[("oT", n, 1)] + 1)
                    if kind == "out" and opens:
                        pe.wait_ge(mT_ready, 2 * layer + 1)
                    if kind == "out" and c0 == 4:
                        pe.wait_ge(mT_ready, 2 * layer + 2)
                    if kind == "br" or (kind == "out" and c0 < 4):
                        sta, first = of(oT_hi, oT_lo), c0
                    elif kind == "out":
                        sta, first = of(hT_hi, hT_lo), c0 - 4
                    else:
                        sta, first = of(hT_hi, hT_lo), c0
                    b0 = pair(j)
                    unit((MIX_AT[layer] + i, 0, 0), [ps[:, b0], ps[:, b0 + 1]], sta, first, opens, closes)
                    while ev and ev[0][0] == i:
                        event(ev.pop(0))

            def ffn(u0, pas, g0, dense):
                tiles = range(TILES if dense else 1)
                gates = [ps[:, 4 + t] for t in tiles]
                ups = [ps[:, 6 + t] for t in tiles] if dense else [ps[:, 5]]
                downs = [[ps[:, 2 * c + t] for t in tiles] for c in range(HALF)] if dense else \
                    [[ps[:, c]] for c in range(HALF)]
                sta = of(hT_hi, hT_lo) if dense else of(xg_hi, xg_lo)
                act_sta = of(aT_hi, aT_lo)

                def steps(f):
                    return pas * FB + (g0 + 0) + f

                def wide(at, step, banks):
                    for k in range(4):
                        unit((u0 + at + k, step, pas), banks, sta, UC * k, k == 0, k == 3)

                def down(at, step, closes=False):
                    for c in range(HALF):
                        for k in range(2):
                            last = unit((u0 + at + 2 * c + k, step, pas), downs[c], act_sta, UC * k, False,
                                        closes and k == 1)
                    return last

                def turn(f):
                    pe.wait_ge(act_done, steps(f) + 1)
                    for t in tiles:
                        for k in range(4):
                            last = nc.tensor.transpose(ups[t][:, k * P:(k + 1) * P], act_s[:, t, k * P:(k + 1) * P],
                                                       ident[:])
                    last.then_inc(aT_filled, 1)

                wide(0, 0, gates)
                if not (isinstance(pas, int) and pas == 0 and g0 == 0):
                    pe.wait_ge(aT_ready, steps(0))
                wide(4, 0, ups)
                if not dense:
                    scatter(pas)
                    for t in range(TILES):
                        last = nc.tensor.transpose(ps[:, 0, t * P:(t + 1) * P], pick_rows[:, t], ident[:])
                    last.then_inc(cols_filled, 1)
                turn(0)
                if not dense:
                    pe.wait_ge(cols_ready, pas + 2)
                for c in range(HALF):
                    for bank in downs[c]:
                        mm(bank, zero_r[:, 0:P], zero_r[:], start=True, stop=False)
                with pe.Fori(1, FB) as f:
                    wide(8, f - 1, gates)
                    pe.wait_ge(aT_ready, steps(f))
                    wide(12, f - 1, ups)
                    down(16, f - 1)
                    turn(f)
                if not dense:
                    gather(pas + 1)
                pe.wait_ge(aT_ready, steps(FB))
                return down(PASS_UNITS - 4, 0, True)

            def gather(pas):
                pe.wait_ge(rows_picked, pas + 1)
                if not isinstance(pas, int):
                    pe.wait_ge(summed, pas * 2)
                for k in range(KC):
                    for t in range(TILES):
                        last = mm(ps[:, 6 + k // 4, (k % 4) * P:(k % 4 + 1) * P], h[:, t, k * P:(k + 1) * P],
                                  pick_rows[:, t], start=t == 0, stop=t == TILES - 1)
                last.then_inc(gathered, 1)

            def scatter(pas):
                pe.wait_ge(yexp_copied, pas + 1)
                pe.wait_ge(cols_ready, pas + 1)
                for t in range(TILES):
                    for c in range(HALF):
                        last = mm(ps[:, 2 + 4 * t + c], pick_cols[:, t * P:(t + 1) * P], y_exp[:, c * NB:(c + 1) * NB],
                                  start=True, stop=True)
                    last.then_inc(scattered, 1)

            norm(0)
            mixer(0)
            close(0)
            norm(1)
            ffn(FFN_AT[0], 0, 0, True)
            close(1)
            norm(2)
            mixer(1)
            close(2)
            norm(3)
            pe.wait_ge(wr_ready, 1)
            for t in range(TILES):
                o = ps[:, 0, t * NE:(t + 1) * NE]
                for k in range(KC):
                    hi, lo = of(hT_hi, hT_lo)(t, k)
                    mm(o, hi, wr_hi[:, k], start=k == 0, stop=False)
                    mm(o, hi, wr_lo[:, k], start=False, stop=False)
                    last = mm(o, lo, wr_hi[:, k], start=False, stop=k == KC - 1)
            last.then_inc(router_done, 1)
            pe.wait_ge(sel_ready, 1)
            chosen = [route[:, 1, t] for t in range(TILES)]
            mm(ps[:, 1, 0:NE], tri_strict[:], chosen[0], start=True, stop=True)
            mm(ps[:, 1, NE:2 * NE], ones[:], chosen[0], start=True, stop=False)
            mm(ps[:, 1, NE:2 * NE], tri_strict[:], chosen[1], start=False, stop=True)
            mm(ps[:, 1, 2 * NE:3 * NE], ones[:], chosen[0], start=True, stop=False)
            mm(ps[:, 1, 2 * NE:3 * NE], ones[:], chosen[1], start=False, stop=True).then_inc(count_done, 1)
            pe.wait_ge(passes_ready, 1)
            for c in range(HALF):
                last = mm(ps[:, c], zero_r[:, 0:P], zero_r[:], start=True, stop=True)
            last.then_inc(yexp_zero, 1)
            gather(0)
            passes = pe.value_load(expert_i[0:1, MAX_OVER:MAX_OVER + 1], min_val=NE, max_val=NE + MAX_OVER)
            with pe.Fori(0, passes) as pas:
                pe.wait_ge(xg_ready, pas + 1)
                ffn(FFN_AT[1], pas, FB, False)
            pe.wait_ge(xg_ready, passes + 1)
            scatter(passes)
            pe.wait_ge(summed, passes * 2 + 2)
            close(3)

        @block.scalar
        def _(act):
            own = Own(act, act_own)
            go = nc.scalar.activation

            def split(u):
                const, step, pas = u
                act.wait_ge(raw_landed[const % RAW], landings(u))
                if not (isinstance(step, int) and isinstance(pas, int) and place(u) < SPLIT):
                    act.wait_ge(unit_used, place(u) - SPLIT + 1)
                go(w_hi[:, const % SPLIT], raw[:, const % RAW], ACT.Copy).then_inc(hi_ready, 1)

            done = [0]

            def split_to(n):
                while done[0] < n:
                    split((done[0], 0, 0))
                    done[0] += 1

            def use_exp_ln():
                nc.scalar.preload_act_table_set("natural_log_exp_and_others")

            def rstd(col, n, width, src, junk):
                own(go(junk, src, ACT.Square, accum_out=stat[:, col:col + 1]))
                own(go(stat[:, col + 4:col + 5], stat[:, col:col + 1], ACT.Ln, bias=eps_col[:, 0:1], scale=1.0 / width))
                go(stat[:, col + 8:col + 9], stat[:, col + 4:col + 5], ACT.Exp, scale=-0.5).then_inc(rstd_ready, 1)

            def close(s):
                for t in range(TILES):
                    y = y_banks(t) if s < 3 else half_rows(y_acc[:, t])
                    own(go(half_rows(h[:, t]), y, ACT.Square, accum_out=stat[:, t:t + 1]))
                own(go(stat[:, 4:6], stat[:, 0:2], ACT.Ln, bias=eps_col[:, 0:1], scale=1.0 / D))
                go(stat[:, 8:10], stat[:, 4:6], ACT.Exp, scale=-0.5).then_inc(rstd_ready, 2)

            def norm(s):
                act.wait_ge(sums_bcast, 1 + 3 * s)
                go(half_rows(mod_shift), ps[:, 4:6], ACT.Copy).then_inc(shift_ready, 1)
                for t in range(TILES):
                    if s:
                        act.wait_ge(x_ready, 2 * (s - 1) + t + 1)
                    elif t == 0:
                        act.wait_ge(x_landed, 16)
                    rstd(2 + t, 0, D, xs[:, t], h[:, t])
                for t in range(TILES):
                    act.wait_ge(hT_filled, 2 * s + t + 1)
                    go(by_tile(hT_hi)[:, t], ps[:, 4 + 2 * t:6 + 2 * t].rearrange("p a (c k) -> p (a c) k", k=P),
                       ACT.Copy).then_inc(hT_half, 1)

            def mixer(layer):
                heads0, uses0 = NH * layer, NT * layer
                base = MIX_AT[layer]

                def job_wait(j):
                    act.wait_ge(unit_used, base + JOB_END[j] + 1)

                def event(e):
                    what = e[1]
                    if what == "logf":
                        act.wait_ge(fpre_ready, layer + 1)
                        own(go(fgate[:, 1], fgate[:, 0], ACT.Abs))
                        own(go(fgate[:, 1], fgate[:, 1], ACT.Exp, scale=-1.0))
                        go(fgate[:, 2], fgate[:, 1], ACT.Ln, bias=one_col[:, 0:1]).then_inc(fsoft_ready, 1)
                    elif what == "lam":
                        act.wait_ge(lam_a, layer + 1)
                        go(lam[:, 2:4], lam[:, 0:2], ACT.Exp).then_inc(lam_b, 1)
                    elif what == "cumT":
                        act.wait_ge(t_filled, uses0 + T_AT[e[1:]] + 1)
                        go(cumT[:], psT[:, 0:SEQ], ACT.Copy).then_inc(t_read, 1)
                    elif what == "evac":
                        j = e[2]
                        kind, n, _ = JOBS[j]
                        job_wait(j)
                        src = ps[:, pair(j):pair(j) + 2]
                        if kind == "v":
                            go(values_in[:, n % 2], src, ACT.Copy).then_inc(job_read, 1)
                        else:
                            go(staged[:], src, ACT.Copy, scale=HEAD ** -0.5 if kind == "q" else 1.0
                               ).then_inc(job_read, 1)
                    elif what == "qkT":
                        _, _, n, qk, t = e
                        act.wait_ge(t_filled, uses0 + T_AT[e[1:]] + 1)
                        go(qkT[:, n % 2, qk, :, t * P:(t + 1) * P], psT.rearrange("p (c k) -> p c k", k=P),
                           ACT.Copy).then_inc(t_read, 1)
                    elif what == "scores" and HEADS[e[2]][0] == SB:
                        k = e[2]
                        act.wait_ge(scores_done, heads0 + k + 1)
                        z = ps[:, 4 + k % 2, 0:3 * P]
                        s = soft[:, k % 2]
                        own(go(s, z, ACT.Abs))
                        own(go(s, s, ACT.Exp, scale=-1.0))
                        go(s, s, ACT.Ln, bias=one_col[:, 0:1]).then_inc(soft_ready, 1)
                    elif what == "exp":
                        k = e[2]
                        branch = HEADS[k][0]
                        before = k - 1 if branch == DIFF else k - 2
                        if before >= 0:
                            act.wait_ge(t_filled, uses0 + T_AT[("probsT", before)] + 1)
                        if branch == SB:
                            act.wait_ge(loga_ready, 8 * layer + k - 7)
                            go(probs[:, k % 2], soft[:, k % 2], ACT.Exp).then_inc(exp_done, 1)
                            return
                        act.wait_ge(max_ready, 12 * layer + (k + 1 if branch == FOX else k - 7))
                        for m in range(2 if branch == DIFF else 1):
                            bank, buf = (4 + m, m) if branch == DIFF else (4 + k % 2, k % 2)
                            for b in range(TILES):
                                at = slice(b * P, b * P + (b + 1) * P)
                                col = 2 * m + b
                                last = go(probs[:, buf, at], ps[:, bank, at], ACT.Exp,
                                          bias=hstat[:, k % 4, col:col + 1],
                                          accum_out=hstat[:, k % 4, 4 + col:5 + col])
                        last.then_inc(exp_done, 1)
                    elif what == "probsT":
                        k = e[2]
                        act.wait_ge(t_filled, uses0 + T_AT[e[1:]] + 1)
                        go(probsT[:, k % 2], psT[:, 0:3 * P], ACT.Copy).then_inc(t_read, 1)
                    elif what == "oT":
                        _, _, n, t = e
                        act.wait_ge(t_filled, uses0 + T_AT[e[1:]] + 1)
                        go(by_tile(oT_hi, 0, 4)[:, t], psT.rearrange("p (c k) -> p c k", k=P), ACT.Copy
                           ).then_inc(t_half, 1)
                    elif what == "diffscale":
                        act.wait_ge(dsum_ready, layer + 1)
                        own(go(dstat[:, 1], dstat[:, 0], ACT.Ln, bias=eps_col[:, 0:1], scale=1.0 / P))
                        go(dstat[:, 1], dstat[:, 1], ACT.Exp, scale=-0.5).then_inc(drstd_ready, 1)
                    elif what == "merge":
                        _, _, n, col = e
                        j = 9 + 4 * n + 2 * col + 1
                        job_wait(j)
                        if n or col:
                            act.wait_ge(merged_ready, 6 * layer + 2 * n + col)
                        go(staged[:], ps[:, pair(j):pair(j) + 2], ACT.Sigmoid).then_inc(job_read, 1)
                    elif what == "mergedT":
                        half = e[2]
                        act.wait_ge(mT_filled, 2 * layer + half + 1)
                        dst = by_tile(hT_hi, 0, 4) if half else by_tile(oT_hi, 0, 4)
                        for t in range(TILES):
                            last = go(dst[:, t], ps[:, 4 + 2 * half + t].rearrange("p (c k) -> p c k", k=P), ACT.Copy)
                        last.then_inc(mT_half, 1)

                act.wait_ge(small_landed, 64 * (layer + 1))
                go(wff_hi[:], wff[:], ACT.Copy).then_inc(wff_half, 1)
                act.wait_ge(mixconst_ready, layer + 1)
                for b in range(4):
                    go(slope_r[:, b], ident[:], ACT.Copy, scale=2.0 ** (-2 * (b + 1)))
                go(dist_r[:], distf[:], ACT.Copy)
                go(mask_r[:], maskf.rearrange("p (m k) -> p m k", m=2), ACT.Copy).then_inc(mask_ready, 1)
                limit = base + MIX_UNITS + (AHEAD if layer == 0 else 0)
                for e in EVENTS:
                    split_to(min(base + e[0] + 1 + AHEAD, limit))
                    event(e)
                split_to(limit)

            def ffn(u0, pas, g0, dense):
                n = TILES if dense else 1
                gates = ps[:, 4:4 + n]
                ups = ps[:, 6:8] if dense else ps[:, 5:6]

                def steps(f):
                    return pas * FB + g0 + f

                def silu(f, at, step):
                    act.wait_ge(unit_used, place((u0 + at, step, pas)))
                    if not (isinstance(f, int) and dense):
                        act.wait_ge(act_done, steps(f))
                    go(gate_s[:, 0:n], gates, ACT.Silu).then_inc(silu_done, 1)

                def turned(f):
                    act.wait_ge(aT_filled, steps(f) + 1)
                    for t in range(n):
                        last = go(by_tile(aT_hi, 0, 4)[:, t], ups[:, t].rearrange("p (c k) -> p c k", k=P), ACT.Copy)
                    last.then_inc(aT_half, 1)

                def splits(at, step, k):
                    for i in range(k):
                        split((u0 + at + i, step, pas))

                if not dense:
                    splits(0, 0, AHEAD)
                    act.wait_ge(unit_used, place((u0, 0, pas)))
                    go(half_rows(y_exp), ps[:, 0:2], ACT.Copy).then_inc(yexp_copied, 1)
                splits(3, 0, 4)
                silu(0, 4, 0)
                splits(7, 0, 4)
                if not dense:
                    act.wait_ge(cols_filled, pas + 1)
                    go(pick_cols[:], ps[:, 0, 0:SEQ], ACT.Copy).then_inc(cols_ready, 1)
                turned(0)
                with act.Fori(1, FB) as f:
                    splits(11, f - 1, 4)
                    silu(f, 12, f - 1)
                    splits(15, f - 1, 8)
                    turned(f)
                splits(PASS_UNITS - 1, 0, 1)
                if not dense:
                    act.wait_ge(gathered, pas + 2)
                    go(by_chunk(xg_hi), ps[:, 6:8], ACT.Copy).then_inc(xg_half, 1)

            act.wait_ge(c_landed, 16)
            go(c_silu[:], c_col[:], ACT.Silu).then_inc(c_ready, 1)
            act.wait_ge(consts_ready, 1)
            go(ident_r[:], ident[:], ACT.Copy).then_inc(idr_ready, 1)
            use_exp_ln()
            norm(0)
            mixer(0)
            use_exp_ln()
            act.wait_ge(unit_used, MIX_UNITS)
            close(0)
            norm(1)
            ffn(FFN_AT[0], 0, 0, True)
            done[0] = FFN_AT[0] + PASS_UNITS
            split_to(MIX_AT[1] + AHEAD)
            use_exp_ln()
            act.wait_ge(unit_used, MIX_AT[1])
            close(1)
            norm(2)
            mixer(1)
            use_exp_ln()
            act.wait_ge(unit_used, FFN_AT[1])
            close(2)
            norm(3)
            act.wait_ge(router_landed, 16)
            go(wr_hi[:], wr[:], ACT.Copy).then_inc(wr_half, 1)
            act.wait_ge(wdiff_ready, 1)
            go(rs[:, 5], rs[:, 4], ACT.Exp).then_inc(wexp_ready, 1)
            act.wait_ge(moeconst_ready, 1)
            go(pick_cols[:], zero_r[:, 0:SEQ].bitcast(F32), ACT.Copy).then_inc(cols_ready, 1)
            act.wait_ge(gathered, 1)
            go(by_chunk(xg_hi), ps[:, 6:8], ACT.Copy).then_inc(xg_half, 1)
            act.wait_ge(yexp_zero, 1)
            act.wait_ge(passes_ready, 1)
            passes = act.value_load(expert_i[0:1, MAX_OVER:MAX_OVER + 1], min_val=NE, max_val=NE + MAX_OVER)
            with act.Fori(0, passes) as pas:
                ffn(FFN_AT[1], pas, FB, False)
            use_exp_ln()
            act.wait_ge(unit_used, passes * PASS_UNITS + FFN_AT[1])
            go(half_rows(y_exp), ps[:, 0:2], ACT.Copy).then_inc(yexp_copied, 1)
            act.wait_ge(summed, passes * 2 + 2)
            close(3)

        @block.vector
        def _(dve):
            own = Own(dve, dve_own)
            tt, ts, stt = nc.vector.tensor_tensor, nc.vector.tensor_scalar, nc.vector.scalar_tensor_tensor
            copy = nc.vector.tensor_copy
            reduce = nc.vector.tensor_reduce

            def split(u):
                dve.wait_ge(hi_ready, place(u) + 1)
                tt(w_lo[:, u[0] % SPLIT], raw[:, u[0] % RAW], w_hi[:, u[0] % SPLIT].bitcast(F32), ALU.subtract
                   ).then_inc(lo_ready, 1)

            done = [0]

            def split_to(n):
                while done[0] < n:
                    split((done[0], 0, 0))
                    done[0] += 1

            def piece(p, s, part, c0, bias=None):
                dve.wait_ge(ada_landed[p[0] % ADA], p[1] * (16 // ADA) + 16 * (p[0] // ADA + 1))
                if not (isinstance(p[1], int) and p[0] == 0):
                    dve.wait_ge(ada_used, p[1] + p[0])
                total = ada_sum[:, region(s, part)]
                if bias is not None:
                    dve.wait_ge(bias_landed, 16 * (bias + 1))
                w = ada_piece[:, p[0] % ADA]
                col = c_silu[:, c0:c0 + 1] if isinstance(c0, int) else c_cur[:, 0:1]
                ins = stt(total, w, col, total if bias is None else ada_bias[:], ALU.mult, ALU.add)
                ins.then_inc(ada_used, 1)
                if bias is not None:
                    dve.wait_ge(ada_used, p[0] + 1)
                    dve.sem_inc(bias_used, 1)

            def close(s):
                dve.wait_ge(sums_bcast, 3 + 3 * s)
                dve.wait_ge(gpost_landed, 16 * (s + 1))
                tt(half_rows(mod_gate), ps[:, 6:8], half_rows(g_post), ALU.mult).then_inc(gate_ready, 1)
                dve.wait_ge(gate_ready, s + 1)
                dve.wait_ge(rstd_ready, 4 + 4 * s)
                for t in range(TILES):
                    y = y_banks(t) if s < 3 else half_rows(y_acc[:, t])
                    own(stt(half_rows(h[:, t]), y, stat[:, 8 + t:9 + t], half_rows(mod_gate), ALU.mult, ALU.mult))
                    tt(xs[:, t], xs[:, t], h[:, t], ALU.add).then_inc(x_ready, 1)

            def norm(s):
                dve.wait_ge(sums_bcast, 2 + 3 * s)
                dve.wait_ge(gpre_landed, 16 * (s + 1))
                stt(half_rows(mod_scale), ps[:, 6:8], 1.0, half_rows(g_pre), ALU.add, ALU.mult).then_inc(scale_ready, 1)
                dve.wait_ge(scale_ready, s + 1)
                dve.wait_ge(shift_ready, s + 1)
                for t in range(TILES):
                    dve.wait_ge(rstd_ready, 4 * s + t + 1)
                    own(stt(h[:, t], xs[:, t], stat[:, 10 + t:11 + t], mod_scale[:], ALU.mult, ALU.mult))
                    tt(h[:, t], h[:, t], mod_shift[:], ALU.add).then_inc(h_ready, 1)
                for t in range(TILES):
                    dve.wait_ge(hT_half, 2 * s + t + 1)
                    tt(by_tile(hT_lo)[:, t], ps[:, 4 + 2 * t:6 + 2 * t].rearrange("p a (c k) -> p (a c) k", k=P),
                       by_tile(hT_hi)[:, t].bitcast(F32), ALU.subtract).then_inc(hT_ready, 1)

            def mixer(layer):
                heads0, uses0 = NH * layer, NT * layer
                base = MIX_AT[layer]

                def event(e):
                    what = e[1]
                    if what == "ff":
                        dve.wait_ge(t_filled, uses0 + T_AT[e[1:]] + 1)
                        tt(fgate[:, 0], psT[:, 0:16].rearrange("p (t n) -> p t n", t=TILES),
                           f_bias[:].unsqueeze(1).to_broadcast([P, TILES, 8]), ALU.add).then_inc(fpre_ready, 1)
                        dve.wait_ge(fpre_ready, layer + 1)
                        dve.sem_inc(t_read, 1)
                    elif what == "lam":
                        own(tt(tail[:, 0:P].rearrange("p (a n) -> p a n", a=2), dl[:, 0::2], dl[:, 1::2], ALU.mult))
                        dve.wait_ge(mixconst_ready, layer + 1)
                        reduce(lam[:, 0:2], tail[:, 0:P].rearrange("p (a n) -> p a n", a=2), AX.X, ALU.add
                               ).then_inc(lam_a, 1)
                        dve.wait_ge(fsoft_ready, layer + 1)
                        stt(fgate[:, 3], fgate[:, 0], 0.0, fgate[:, 2], ALU.min, ALU.subtract).then_inc(logf_ready, 1)
                    elif what == "cum":
                        dve.wait_ge(t_filled, uses0 + T_AT[e[1:]] + 1)
                        src = psT[:, 0:16].rearrange("p (t n) -> p t n", t=TILES)
                        copy(cum[:, :, 0:8], src)
                        own(ts(cum[:, :, 8:16], src, -1.0, None, ALU.mult))
                        dve.sem_inc(cumrows_ready, 1)
                        dve.sem_inc(t_read, 1)
                    elif what == "lam2":
                        dve.wait_ge(lam_b, layer + 1)
                        own(tt(lam[:, 4:5], lam[:, 3:4], lam[:, 2:3], ALU.subtract))
                        own(ts(lam[:, 5:6], lam[:, 4:5], -lam_init[layer], None, ALU.add))
                        own(ts(subln[:], subln[:], 1.0 - lam_init[layer], None, ALU.mult))
                    elif what == "scores":
                        k = e[2]
                        branch = HEADS[k][0]
                        if branch == SB:
                            dve.wait_ge(soft_ready, 8 * layer + k - 7)
                            z = ps[:, 4 + k % 2, 0:3 * P]
                            own(stt(stay[:], z, 0.0, soft[:, k % 2], ALU.max, ALU.add))
                            for b in range(TILES):
                                at = slice(b * P, b * P + (b + 1) * P)
                                last = nc.vector.tensor_tensor_scan(tail[:, at][:, ::-1], stay[:, at][:, ::-1],
                                                                    zeros[:, 0:(b + 1) * P], 0.0, ALU.add, ALU.add)
                            own(last)
                            tt(soft[:, k % 2], z, tail[:], ALU.subtract).then_inc(loga_ready, 1)
                            return
                        dve.wait_ge(scores_done, heads0 + k + 1)
                        for b in range(TILES):
                            at = slice(b * P, b * P + (b + 1) * P)
                            if branch == DIFF:
                                last = reduce(hstat[:, k % 4, b:4:2], ps[:, 4:6, at], AX.X, ALU.max, negate=True)
                            else:
                                last = reduce(hstat[:, k % 4, b:b + 1], ps[:, 4 + k % 2, at], AX.X, ALU.max, negate=True)
                        last.then_inc(max_ready, 1)
                    elif what == "combine":
                        k = e[2]
                        s = hstat[:, k % 4]
                        dve.wait_ge(exp_done, heads0 + k + 1)
                        own(nc.vector.reciprocal(s[:, 8:12], s[:, 4:8]))
                        own(ts(s[:, 10:12], s[:, 10:12], lam[:, 5:6], None, ALU.mult))
                        for b in range(TILES):
                            at = slice(b * P, b * P + (b + 1) * P)
                            last = ts(probs[:, 1, at], probs[:, 1, at], s[:, 10 + b:11 + b], None, ALU.mult)
                        own(last)
                        for b in range(TILES):
                            at = slice(b * P, b * P + (b + 1) * P)
                            last = stt(probs[:, 0, at], probs[:, 0, at], s[:, 8 + b:9 + b], probs[:, 1, at],
                                       ALU.mult, ALU.add)
                        last.then_inc(comb_done, 1)
                    elif what == "values":
                        k = e[2]
                        branch, hd = HEADS[k]
                        width, at = (P, (k % 2) * 2 * P) if branch == DIFF else (HEAD, (k % 4) * P)
                        src = psO[:, at:at + 2 * width].rearrange("p (t n) -> p t n", t=TILES)
                        dst = o_rows[:, branch % 2, :, hd * width:(hd + 1) * width]
                        if branch == FOX:
                            s = hstat[:, k % 4]
                            dve.wait_ge(exp_done, heads0 + k + 1)
                            own(nc.vector.reciprocal(s[:, 8:10], s[:, 4:6]))
                            dve.wait_ge(values_done, heads0 + k + 1)
                            tt(dst, src, s[:, 8:10].unsqueeze(2).to_broadcast([P, TILES, HEAD]), ALU.mult
                               ).then_inc(o_ready, 1)
                        else:
                            dve.wait_ge(values_done, heads0 + k + 1)
                            copy(dst, src).then_inc(o_ready, 1)
                    elif what == "diffnorm":
                        dve.wait_ge(o_ready, heads0 + NH)
                        own(tt(values_in[:, 1], o_rows[:, 0], o_rows[:, 0], ALU.mult))
                        reduce(dstat[:, 0], values_in[:, 1].rearrange("p t (n k) -> p (t n) k", k=P), AX.X, ALU.add
                               ).then_inc(dsum_ready, 1)
                    elif what == "diffscale":
                        dve.wait_ge(drstd_ready, layer + 1)
                        o = o_rows[:, 0].rearrange("p t (n k) -> p (t n) k", k=P)
                        own(tt(o, o, dstat[:, 1].unsqueeze(2).to_broadcast([P, 8, P]), ALU.mult))
                        tt(o, o, subln[:].unsqueeze(1).to_broadcast([P, 8, P]), ALU.mult).then_inc(dscaled, 1)
                    elif what == "oT":
                        _, _, n, t = e
                        dve.wait_ge(t_half, 6 * layer + 2 * n + t + 1)
                        tt(by_tile(oT_lo, 0, 4)[:, t], psT.rearrange("p (c k) -> p c k", k=P),
                           by_tile(oT_hi, 0, 4)[:, t].bitcast(F32), ALU.subtract).then_inc(t_read, 1)
                    elif what == "merge":
                        _, _, n, col = e
                        j = 9 + 4 * n + 2 * col
                        dve.wait_ge(job_read, job_reads(layer, j + 1))
                        br = ps[:, pair(j):pair(j) + 2]
                        dst = h[:, :, col * NB:(col + 1) * NB]
                        if n == 0:
                            tt(dst, br, staged[:], ALU.mult).then_inc(merged_ready, 1)
                        else:
                            own(tt(staged[:], br, staged[:], ALU.mult))
                            tt(dst, dst, staged[:], ALU.add).then_inc(merged_ready, 1)
                    elif what == "mergedT":
                        half = e[2]
                        dve.wait_ge(mT_half, 2 * layer + half + 1)
                        hi, lo = (hT_hi, hT_lo) if half else (oT_hi, oT_lo)
                        for t in range(TILES):
                            last = tt(by_tile(lo, 0, 4)[:, t], ps[:, 4 + 2 * half + t].rearrange("p (c k) -> p c k", k=P),
                                      by_tile(hi, 0, 4)[:, t].bitcast(F32), ALU.subtract)
                        last.then_inc(mT_ready, 1)

                dve.wait_ge(wff_half, layer + 1)
                tt(wff_lo[:], wff[:], wff_hi[:].bitcast(F32), ALU.subtract).then_inc(wff_ready, 1)
                limit = base + MIX_UNITS + (AHEAD if layer == 0 else 0)
                p = 0
                for i in range(MIX_UNITS):
                    split_to(min(base + i + 1 + AHEAD, limit))
                    for e in EVENTS:
                        if e[0] == i:
                            event(e)
                    while p < MIX_PIECES and PIECE_AT[p] <= i:
                        s, part = ADA_MIX[layer][p // KC]
                        piece((PIECE0[2 * layer] + p, 0), s, part, p % KC,
                              BIAS0[2 * layer] + p // KC if p % KC == 0 else None)
                        p += 1

            def ffn(u0, pas, g0, dense):
                n = TILES if dense else 1
                ups = ps[:, 6:8] if dense else ps[:, 5:6]

                def steps(f):
                    return pas * FB + g0 + f

                def splits(at, step, k):
                    for i in range(k):
                        split((u0 + at + i, step, pas))

                def product(f, at, step):
                    dve.wait_ge(silu_done, steps(f) + 1)
                    dve.wait_ge(unit_used, place((u0 + at, step, pas)))
                    tt(act_s[:, 0:n], gate_s[:, 0:n], ups, ALU.mult).then_inc(act_done, 1)

                def turned(f):
                    dve.wait_ge(aT_half, steps(f) + 1)
                    for t in range(n):
                        last = tt(by_tile(aT_lo, 0, 4)[:, t], ups[:, t].rearrange("p (c k) -> p c k", k=P),
                                  by_tile(aT_hi, 0, 4)[:, t].bitcast(F32), ALU.subtract)
                    last.then_inc(aT_ready, 1)

                if not dense:
                    splits(0, 0, AHEAD)
                splits(3, 0, 4)
                if dense:
                    for part in range(2):
                        piece((PIECE0[1] + part, 0), 2, part, 0, BIAS0[1] + part)
                splits(7, 0, 4)
                product(0, 8, 0)
                if not dense:
                    gather_sum(pas)
                turned(0)
                if not dense:
                    pick(pas + 1)
                with dve.Fori(1, FB) as f:
                    splits(11, f - 1, 4)
                    if dense:
                        copy(c_cur[:], c_silu[:, bass.ds(f, 1)]).then_inc(ccur_ready, 1)
                        dve.wait_ge(ccur_ready, f)
                        for part in range(2):
                            piece((PIECE0[1] + 2 + part, (f - 1) * 2), 2, part, f)
                    splits(15, f - 1, 4)
                    product(f, 16, f - 1)
                    splits(19, f - 1, 4)
                    turned(f)
                splits(PASS_UNITS - 1, 0, 1)
                if dense:
                    for part in range(2):
                        piece((PIECE0[1] + 14 + part, 0), 2, part, KC - 1)
                else:
                    dve.wait_ge(xg_half, pas + 2)
                    gathered_low()

            def gathered_low():
                tt(by_chunk(xg_lo), ps[:, 6:8], by_chunk(xg_hi).bitcast(F32), ALU.subtract).then_inc(xg_ready, 1)

            def gather_sum(pas):
                at = table[:, bass.ds(pas, 1)] if not isinstance(pas, int) else table[:, pas:pas + 1]
                copy(cur_w[:], at.rearrange("p o q t -> p (o q) t")[:, 2]).then_inc(curw_ready, 1)
                dve.wait_ge(curw_ready, pas + 1)
                for t in range(TILES):
                    dve.wait_ge(scattered, pas * 2 + t + 1)
                    dst = half_rows(y_acc[:, t])
                    stt(dst, ps[:, 2 + 4 * t:4 + 4 * t], cur_w[:, t:t + 1], dst, ALU.mult, ALU.add).then_inc(summed, 1)

            def pick(pas):
                at = table[:, bass.ds(pas + 1, 1)] if not isinstance(pas, int) else table[:, pas + 1:pas + 2]
                if not isinstance(pas, int):
                    dve.wait_ge(cols_filled, pas)
                copy(cur[:], at.rearrange("p o q t -> p (o q) t")).then_inc(cur_ready, 1)
                dve.wait_ge(cur_ready, pas + 1)
                for t in range(TILES):
                    last = ts(pick_rows[:, t], slots[:], cur[:, 0, t:t + 1], cur[:, 1, t:t + 1], ALU.is_equal, ALU.mult)
                last.then_inc(rows_picked, 1)

            def routing():
                bc = lambda col: col.unsqueeze(2).to_broadcast([P, TILES, NE])
                own(copy(rt[:, 0], ps[:, 0, 0:2 * NE].rearrange("p (t e) -> p t e", t=TILES)))
                for a in range(2):
                    logits, equal, first, hot = rt[:, 5 * a], rt[:, 5 * a + 1], rt[:, 5 * a + 2], rt[:, 5 * a + 3]
                    own(reduce(rs[:, 2 * a], logits, AX.X, ALU.max))
                    own(tt(equal, logits, bc(rs[:, 2 * a]), ALU.is_equal))
                    own(tt(first, equal, rank[:], ALU.mult))
                    own(reduce(rs[:, 2 * a + 1], first, AX.X, ALU.max))
                    own(tt(hot, first, bc(rs[:, 2 * a + 1]), ALU.is_equal))
                    if a == 0:
                        own(stt(rt[:, 5], hot, FAR, logits, ALU.mult, ALU.add))
                tt(rs[:, 4], rs[:, 2], rs[:, 0], ALU.subtract).then_inc(wdiff_ready, 1)
                tt(route[:, 1], rt[:, 3], rt[:, 8], ALU.add).then_inc(sel_ready, 1)
                dve.wait_ge(wexp_ready, 1)
                own(ts(rs[:, 6], rs[:, 5], 1.0, None, ALU.add))
                own(nc.vector.reciprocal(rs[:, 7], rs[:, 6]))
                own(tt(rs[:, 8], rs[:, 5], rs[:, 7], ALU.mult))
                tt(rt[:, 4], rt[:, 3], bc(rs[:, 7]), ALU.mult)
                own(tt(rt[:, 9], rt[:, 8], bc(rs[:, 8]), ALU.mult))
                tt(route[:, 2], rt[:, 4], rt[:, 9], ALU.add)
                dve.wait_ge(count_done, 1)
                copy(route[:, 0], ps[:, 1, 0:2 * NE].rearrange("p (t e) -> p t e", t=TILES))
                own(ts(rt[:, 10, 0], ps[:, 1, 2 * NE:3 * NE], float(P), None, ALU.is_gt))
                own(nc.vector.tensor_tensor_scan(rt[:, 11, 0], rt[:, 10, 0], zero_r[:, 0:NE].bitcast(F32), 0.0,
                                                 ALU.add, ALU.add))
                own(ts(expert_f[:, MAX_OVER:MAX_OVER + 1], rt[:, 11, 0, NE - 1:NE], float(NE), None, ALU.add))
                flat = route.rearrange("p q t e -> p (q t) e")
                own(copy(table[:, 1:1 + NE].rearrange("p e q t -> p e (q t)"), flat.rearrange("p q e -> p e q")))
                for j in range(MAX_OVER):
                    own(stt(rt[:, 12 + j, 0], rt[:, 11, 0], float(j + 1), rt[:, 10, 0], ALU.is_equal, ALU.mult))
                    own(tt(rt[:, 12 + j, 1], rt[:, 12 + j, 0], index[:], ALU.mult))
                    own(reduce(expert_f[:, j:j + 1], rt[:, 12 + j, 1], AX.X, ALU.add))
                    own(tt(rt[:, 16:19].rearrange("p q t e -> p (q t) e"), flat,
                           rt[:, 12 + j, 0].unsqueeze(1).to_broadcast([P, 3 * TILES, NE]), ALU.mult))
                    own(reduce(table[:, 1 + NE + j].rearrange("p q t -> p (q t)"),
                               rt[:, 16:19].rearrange("p q t e -> p (q t) e"), AX.X, ALU.add))
                    own(ts(table[:, 1 + NE + j, 0], table[:, 1 + NE + j, 0], -float(P), None, ALU.add))
                own(copy(expert_i[:, 0:MAX_OVER + 1], expert_f[:, 0:MAX_OVER + 1]))
                dve.sem_inc(passes_ready, 1)

            dve.wait_ge(c_ready, 1)
            own(nc.vector.memset(zero_r[:].bitcast(F32), 0.0))
            for k in range(KC):
                dve.wait_ge(start_landed[k], 16)
                for part in range(2):
                    if k:
                        dve.wait_ge(start_used, 2 * (k - 1) + part + 1)
                    else:
                        dve.wait_ge(bias_landed, 16 * (part + 1))
                    stt(ada_sum[:, part], ada_start[:, k, part], c_silu[:, k:k + 1],
                        ada_sum[:, part] if k else ada_bias[:], ALU.mult, ALU.add).then_inc(start_used, 1)
                    if k == 0:
                        dve.wait_ge(start_used, part + 1)
                        dve.sem_inc(bias_used, 1)
            norm(0)
            mixer(0)
            close(0)
            norm(1)
            ffn(FFN_AT[0], 0, 0, True)
            done[0] = FFN_AT[0] + PASS_UNITS
            split_to(MIX_AT[1] + AHEAD)
            close(1)
            norm(2)
            mixer(1)
            close(2)
            norm(3)
            dve.wait_ge(wr_half, 1)
            tt(wr_lo[:], wr[:], wr_hi[:].bitcast(F32), ALU.subtract).then_inc(wr_ready, 1)
            dve.wait_ge(moeconst_ready, 1)
            dve.wait_ge(router_done, 1)
            routing()
            pick(0)
            dve.wait_ge(xg_half, 1)
            gathered_low()
            passes = dve.value_load(expert_i[0:1, MAX_OVER:MAX_OVER + 1], min_val=NE, max_val=NE + MAX_OVER)
            with dve.Fori(0, passes) as pas:
                ffn(FFN_AT[1], pas, FB, False)
            gather_sum(passes)
            close(3)


_INS = ["x", "c", "w_ada", "b_ada", "norm_g", "w_in", "fox_f_bias", "diff_lambda", "diff_subln_g", "w_branch",
        "w_out", "ffn_w_gate", "ffn_w_up", "ffn_w_down", "moe_router", "moe_w_gate", "moe_w_up", "moe_w_down"]
_OUTS = [((1, SEQ, D), "float32")]


def kernel(**inputs):
    import numpy as _np
    import concourse.bacc as _bacc
    from concourse import mybir as _mybir
    from concourse.bass_utils import run_bass_kernel_spmd as _run

    nc = _bacc.Bacc("TRN2", target_bir_lowering=False, num_devices=1, dynamic_dma_scratch_size=1024)
    arrays, args = {}, []
    for name in _INS:
        a = _np.ascontiguousarray(inputs[name])
        arrays[f"in_{name}_dram"] = a
        args.append(nc.dram_tensor(f"in_{name}_dram", a.shape, _mybir.dt.from_np(a.dtype), kind="ExternalInput").ap())
    for i, (shape, dtype) in enumerate(_OUTS):
        dt = _mybir.dt.from_np(_np.dtype(dtype))
        args.append(nc.dram_tensor(f"out_{i}_dram", shape, dt, kind="ExternalOutput").ap())
    build(nc, *args)
    r = _run(nc, [arrays], core_ids=[0])
    return r.results[0]["out_0_dram"]
```

```python
import math
from contextlib import ExitStack

import concourse.bass as bass
from concourse import mybir

F32 = mybir.dt.float32
F32R = mybir.dt.float32r
I32 = mybir.dt.int32
ACT = mybir.ActivationFunctionType
ALU = mybir.AluOpType
AX = mybir.AxisListType

P = 128
D = 1024
SEQ = 256
TILES = SEQ // P
KC = D // P
HEAD = 64
NE = 8
FFN = 3584
NB = 512
UC = 2
FB = FFN // NB
HALF = D // NB
FOX, SB, DIFF = range(3)
EPS = 1e-6
MASKED = -float(2 ** 100)
FAR = -1e38

RAW = 6
DEEP = 12
SPLIT = 4
AHEAD = SPLIT - 1
ADA = 2

MIX_UNITS = 80
STEP_UNITS = 12
PASS_UNITS = STEP_UNITS * FB
MAX_OVER = 3
COLS = 1 + NE + MAX_OVER + 1

W_OFF = {}
_at = 0
for _name, _w in (("q0", 512), ("k0", 512), ("v0", 512), ("ff", 8), ("q1", 512), ("k1", 512),
                  ("v1", 512), ("q2", 512), ("k2", 512), ("v2", 512), ("gl", 3 * D)):
    W_OFF[_name] = _at
    _at += _w

JOBS = [(kind, n, 0) for n in range(3) for kind in "qkv"]
for _n in range(3):
    for _c in range(HALF):
        JOBS += [("gl", _n, _c), ("br", _n, _c)]
JOBS += [("out", 0, 1), ("out", 0, 0)]
UNITS = []
for _j, (_kind, _n, _c) in enumerate(JOBS[:-2]):
    _k = 4 if _kind == "br" else KC
    UNITS += [(_j, c, c == 0, c + UC == _k) for c in range(0, _k, UC)]
for _lo in (0, 4):
    for _c in range(HALF):
        UNITS += [(len(JOBS) - 2 + _c, c, c == 0, c + UC == KC) for c in (_lo, _lo + UC)]
assert len(UNITS) == MIX_UNITS
JOB_END = {u[0]: i for i, u in enumerate(UNITS)}

HEADS = [(FOX, h) for h in range(8)] + [(SB, h) for h in range(8)] + [(DIFF, h) for h in range(4)]
SCORE_AT = [13, 14, 16, 17, 19, 20, 22, 23] + [26, 27, 29, 30, 32, 33, 35, 36] + [39, 42, 45, 48]


def mixer_events():
    ev = [(0, "wff"), (3, "ff"), (4, "logf"), (4, "lam"), (5, "lam2"), (6, "consts"), (7, "cum"), (10, "cumT")]
    for n in range(3):
        e = 12 * n
        ev += [(e + 3, "evac", 3 * n), (e + 7, "evac", 3 * n + 1), (e + 11, "evac", 3 * n + 2)]
    for k, at in enumerate(SCORE_AT):
        late = HEADS[k][0] == DIFF
        ev += [(at, "scores", k), (at + 1, "exp", k), (at + 3 + late, "probsT", k), (at + 5 + late, "values", k)]
        if late:
            ev.append((at + 2, "combine", k))
    for at, what in zip((5, 6, 8, 9, 17, 18, 21, 24, 28, 29, 34, 37),
                        [(n, qk, t) for n in range(3) for qk in range(2) for t in range(2)]):
        ev.append((at, "qkT") + what)
    ev += [(31, "oT", 0, 0), (38, "oT", 0, 1), (48, "oT", 1, 0), (50, "oT", 1, 1)]
    ev += [(55, "diffnorm"), (56, "diffscale"), (60, "oT", 2, 0), (62, "oT", 2, 1)]
    for n in range(3):
        for c in range(HALF):
            ev.append((JOB_END[9 + 4 * n + 2 * c], "gates", n, c))
            ev.append((JOB_END[9 + 4 * n + 2 * c + 1], "merge", n, c))
    ev += [(69, "mergedT", 0), (73, "mergedT", 1)]
    ev.append((GATE_AT, "gate"))
    order = {"evac": 0, "gates": 0, "merge": 0, "values": 2, "probsT": 3, "oT": 4, "qkT": 5, "scores": 6}
    return sorted(ev, key=lambda x: (x[0], order.get(x[1], 1)))


GATE_AT = MIX_UNITS - 4
EVENTS = mixer_events()
T_USES = [e[1:] for e in EVENTS if e[1] in ("ff", "cum", "cumT", "qkT", "probsT", "oT")]
T_AT = {key: i for i, key in enumerate(T_USES)}
NT = len(T_USES)
NH = len(HEADS)

ADA_MIX = {0: [(0, 2), (1, 0), (1, 1), (1, 2)], 1: [(2, 2), (3, 0), (3, 1), (3, 2)]}
MIX_PIECES = 4 * KC
FFN_PIECES = 2 * KC
PIECE_AT = [2 + 2 * i for i in range(MIX_PIECES)]
PIECE_LEAD = AHEAD + 2


def region(s, part):
    return part if part < 2 else 2 + s % 2


def build(nc, x, c, w_ada, b_ada, norm_g, w_in, fox_f_bias, diff_lambda, diff_subln_g, w_branch,
          w_out, ffn_w_gate, ffn_w_up, ffn_w_down, moe_router, moe_w_gate, moe_w_up, moe_w_down, out):
    lam_init = [0.8 - 0.6 * math.exp(-0.3 * layer) for layer in range(2)]
    ctx = ExitStack()
    with ctx:
        def sb(name, shape, dt=F32, into=ctx):
            return into.enter_context(nc.sbuf_tensor(name, shape, dt))

        def sem(name):
            return ctx.enter_context(nc.semaphore(name))

        xs = sb("xs", [P, TILES, D])
        h = sb("h", [P, TILES, D])
        hT_hi = sb("hT_hi", [P, KC, SEQ], F32R)
        hT_lo = sb("hT_lo", [P, KC, SEQ], F32R)
        raw = sb("raw", [P, RAW, UC, NB])
        w_hi = sb("w_hi", [P, SPLIT, UC, NB], F32R)
        w_lo = sb("w_lo", [P, SPLIT, UC, NB], F32R)
        ada_piece = sb("ada_piece", [P, ADA, D])
        ada_sum = sb("ada_sum", [P, 4, D])
        ada_bias = sb("ada_bias", [P, D])
        mod_scale = sb("mod_scale", [P, D])
        mod_shift = sb("mod_shift", [P, D])
        mod_gate = sb("mod_gate", [P, D])
        mod_junk = sb("mod_junk", [P, D])
        g_pre = sb("g_pre", [P, D])
        g_post = sb("g_post", [P, D])
        c_col = sb("c_col", [P, KC])
        c_silu = sb("c_silu", [P, KC])
        ident = sb("ident", [P, P])
        ident_r = sb("ident_r", [P, P], F32R)
        ones = sb("ones", [P, P])
        tri = sb("tri", [P, P])
        tri_strict = sb("tri_strict", [P, P])
        stat = sb("stat", [P, 16])
        zero_r = sb("zero_r", [P, NB], F32R)
        c_cur = sb("c_cur", [P, 1])
        eps_col = sb("eps_col", [P, 1])
        one_col = sb("one_col", [P, 1])

        mix = ExitStack()
        values_in = sb("values_in", [P, 2, TILES, NB], into=mix)
        qkT = sb("qkT", [P, 2, 2, 4, SEQ], into=mix)
        staged = sb("staged", [P, TILES, NB], into=mix)
        oT_hi = sb("oT_hi", [P, 4, SEQ], F32R, into=mix)
        oT_lo = sb("oT_lo", [P, 4, SEQ], F32R, into=mix)
        o_rows = sb("o_rows", [P, 2, TILES, NB], into=mix)
        probs = sb("probs", [P, 2, 3 * P], into=mix)
        probsT = sb("probsT", [P, 2, 3 * P], into=mix)
        soft = sb("soft", [P, 2, 3 * P], into=mix)
        stay = sb("stay", [P, 3 * P], into=mix)
        tail = sb("tail", [P, 3 * P], into=mix)
        dist_r = sb("dist_r", [P, 3 * P], F32R, into=mix)
        slope_r = sb("slope_r", [P, 4, P], F32R, into=mix)
        mask_r = sb("mask_r", [P, 2, P], F32R, into=mix)
        maskf = sb("maskf", [P, 2 * P], into=mix)
        distf = sb("distf", [P, 3 * P], into=mix)
        zeros = sb("zeros", [P, SEQ], into=mix)
        wff = sb("wff", [P, KC, 8], into=mix)
        wff_split = sb("wff_split", [P, KC, 2, 8], F32R, into=mix)
        f_bias = sb("f_bias", [P, 8], into=mix)
        fgate = sb("fgate", [P, 4, TILES, 8], into=mix)
        cum = sb("cum", [P, TILES, P], into=mix)
        cumT = sb("cumT", [P, SEQ], into=mix)
        cum_mov = sb("cum_mov", [P, SEQ], F32R, into=mix)
        cum_sta = sb("cum_sta", [P, 2, SEQ], F32R, into=mix)
        cum_split = sb("cum_split", [P, TILES, 16], F32R, into=mix)
        own_rows = sb("own_rows", [P, 2, 8], into=mix)
        pick = sb("pick", [P, 2], into=mix)
        dl = sb("dl", [P, 4, HEAD], into=mix)
        lam = sb("lam", [P, 8], into=mix)
        subln = sb("subln", [P, P], into=mix)
        hstat = sb("hstat", [P, 4, 12], into=mix)
        dstat = sb("dstat", [P, 2, 8], into=mix)
        mix.close()
        start_stack = ExitStack()
        ada_start = sb("ada_start", [P, KC, 2, D], into=start_stack)
        start_stack.close()
        ffn_stack = ExitStack()
        aT_hi = sb("aT_hi", [P, 4, SEQ], F32R, into=ffn_stack)
        aT_lo = sb("aT_lo", [P, 4, SEQ], F32R, into=ffn_stack)
        gate_s = sb("gate_s", [P, TILES, NB], into=ffn_stack)
        act_s = sb("act_s", [P, TILES, NB], into=ffn_stack)
        xg_hi = sb("xg_hi", [P, KC, P], F32R, into=ffn_stack)
        xg_lo = sb("xg_lo", [P, KC, P], F32R, into=ffn_stack)
        y_acc = sb("y_acc", [P, TILES, D], into=ffn_stack)
        y_exp = sb("y_exp", [P, D], into=ffn_stack)
        raw_more = sb("raw_more", [P, DEEP - RAW, UC, NB], into=ffn_stack)
        pick_rows = sb("pick_rows", [P, TILES, P], into=ffn_stack)
        pick_cols = sb("pick_cols", [P, SEQ], into=ffn_stack)
        slots = sb("slots", [P, P], into=ffn_stack)
        wr = sb("wr", [P, KC, NE], into=ffn_stack)
        wr_split = sb("wr_split", [P, KC, 2, NE], F32R, into=ffn_stack)
        rt = sb("rt", [P, 20, TILES, NE], into=ffn_stack)
        route = sb("route", [P, 3, TILES, NE], into=ffn_stack)
        rank = sb("rank", [P, TILES, NE], into=ffn_stack)
        index = sb("index", [P, NE], into=ffn_stack)
        rs = sb("rs", [P, 16, TILES], into=ffn_stack)
        table = sb("table", [P, COLS, 3, TILES], into=ffn_stack)
        cur = sb("cur", [P, 3, TILES], into=ffn_stack)
        cur_w = sb("cur_w", [P, TILES], into=ffn_stack)
        expert_f = sb("expert_f", [P, 16], into=ffn_stack)
        expert_i = sb("expert_i", [P, 16], I32, into=ffn_stack)
        ffn_stack.close()

        ps = ctx.enter_context(nc.psum_tensor("ps", [P, 8, NB], F32))
        psT = ps[:, 6]
        psO = ps[:, 7]

        raw_landed = [sem(f"raw_landed{i}") for i in range(DEEP)]
        hi_ready, lo_ready, unit_used = sem("hi_ready"), sem("lo_ready"), sem("unit_used")
        ada_landed = [sem(f"ada_landed{i}") for i in range(ADA)]
        ada_used, bias_landed, bias_used = sem("ada_used"), sem("bias_landed"), sem("bias_used")
        start_landed = [sem(f"start_landed{i}") for i in range(KC)]
        start_used, x_landed, c_landed = sem("start_used"), sem("x_landed"), sem("c_landed")
        small_landed, gpre_landed, gpost_landed = sem("small_landed"), sem("gpre_landed"), sem("gpost_landed")
        router_landed, consts_ready, mixconst_ready = sem("router_landed"), sem("consts_ready"), sem("mixconst_ready")
        mask_ready, c_ready = sem("mask_ready"), sem("c_ready")
        sums_bcast, gate_ready, shift_ready, scale_ready = (
            sem("sums_bcast"), sem("gate_ready"), sem("shift_ready"), sem("scale_ready"))
        y_squared, y_scaled, y_summed = sem("y_squared"), sem("y_scaled"), sem("y_summed")
        rstd_ready, x_ready, h_ready = sem("rstd_ready"), sem("x_ready"), sem("h_ready")
        hT_filled, hT_half, hT_ready = sem("hT_filled"), sem("hT_half"), sem("hT_ready")
        job_read, merged_ready = sem("job_read"), sem("merged_ready")
        wff_half, wff_ready = sem("wff_half"), sem("wff_ready")
        fpre_ready, fsoft_ready, logf_ready = sem("fpre_ready"), sem("fsoft_ready"), sem("logf_ready")
        cumrows_ready, cumsta_ready = sem("cumrows_ready"), sem("cumsta_ready")
        scores_done, max_ready, exp_done, comb_done = (
            sem("scores_done"), sem("max_ready"), sem("exp_done"), sem("comb_done"))
        soft_ready, loga_ready = sem("soft_ready"), sem("loga_ready")
        t_filled, t_half, t_read = sem("t_filled"), sem("t_half"), sem("t_read")
        values_done, o_ready = sem("values_done"), sem("o_ready")
        mT_filled, mT_half, mT_ready = sem("mT_filled"), sem("mT_half"), sem("mT_ready")
        lam_a, lam_b = sem("lam_a"), sem("lam_b")
        dsum_ready, drstd_ready, dscaled = sem("dsum_ready"), sem("drstd_ready"), sem("dscaled")
        silu_done, act_done, ccur_ready = sem("silu_done"), sem("act_done"), sem("ccur_ready")
        aT_filled, aT_half, aT_ready = sem("aT_filled"), sem("aT_half"), sem("aT_ready")
        yexp_copied = sem("yexp_copied")
        wr_half, wr_ready = sem("wr_half"), sem("wr_ready")
        router_done, wdiff_ready, wexp_ready, sel_ready = (
            sem("router_done"), sem("wdiff_ready"), sem("wexp_ready"), sem("sel_ready"))
        count_read = sem("count_read")
        count_done, passes_ready, moeconst_ready = sem("count_done"), sem("passes_ready"), sem("moeconst_ready")
        rows_picked, cols_filled, cols_ready = sem("rows_picked"), sem("cols_filled"), sem("cols_ready")
        gathered, xg_half, xg_ready = sem("gathered"), sem("xg_half"), sem("xg_ready")
        scattered = [sem(f"scattered{t}") for t in range(TILES)]
        summed, cur_ready, curw_ready = sem("summed"), sem("cur_ready"), sem("curw_ready")
        act_own, dve_own, pool_own, stored = sem("act_own"), sem("dve_own"), sem("pool_own"), sem("stored")

        class Own:

            def __init__(self, eng, s):
                self.eng, self.s, self.n = eng, s, 0

            def __call__(self, ins):
                self.n += 1
                ins.then_inc(self.s, 1)
                self.eng.wait_ge(self.s, self.n)

        MIX_AT = [0, MIX_UNITS + PASS_UNITS]
        FFN_AT = [MIX_UNITS, 2 * MIX_UNITS + PASS_UNITS]
        PIECE0 = [0, MIX_PIECES, MIX_PIECES + FFN_PIECES]
        BIAS0 = [2, 6, 8]
        GATE_PIECES = [KC, MIX_PIECES, MIX_PIECES + FFN_PIECES + KC]
        MOD_PIECES = [0, 3 * KC, MIX_PIECES + FFN_PIECES, MIX_PIECES + FFN_PIECES + 3 * KC]

        def place(u):
            const, step, pas = u
            return step * STEP_UNITS + pas * PASS_UNITS + const

        def raw_slot(u):
            s = u[0] % (DEEP if u[0] >= FFN_AT[1] else RAW)
            return s, raw[:, s] if s < RAW else raw_more[:, s - RAW]

        def landings(u):
            const, step, pas = u
            if const < FFN_AT[1]:
                return step * (16 * STEP_UNITS // RAW) + pas * (16 * PASS_UNITS // RAW) + 16 * (const // RAW + 1)
            s = const % DEEP
            before = (FFN_AT[1] - 1 - s) // RAW + 1 if s < RAW else 0
            first = FFN_AT[1] + (s - FFN_AT[1]) % DEEP
            return (step * (16 * STEP_UNITS // DEEP) + pas * (16 * PASS_UNITS // DEEP)
                    + 16 * (before + (const - first) // DEEP + 1))

        def chunks(w):
            return w.rearrange("(c p) n -> p c n", p=P)

        def unit_source(layer, i):
            j, c0, _, _ = UNITS[i]
            kind, n, col = JOBS[j]
            if kind == "br":
                w, at = w_branch[layer, n], NB * col
            elif kind == "out":
                w, at = w_out[layer], NB * col
            elif kind == "gl":
                w, at = w_in[layer], W_OFF["gl"] + n * D + NB * col
            else:
                w, at = w_in[layer], W_OFF[f"{kind}{n}"]
            return chunks(w)[:, c0:c0 + UC, at:at + NB]

        def pair(j):
            return (j % 2) * 2 if j < len(JOBS) - 2 else 2 * JOBS[j][2]

        def half_rows(tile, n0=0):
            return tile.rearrange("p (a n) -> p a n", a=HALF)

        def y_block(s, i, t):
            c = i if s % 2 else 1 - i
            return ps[:, 2 * c + t], slice(c * NB, (c + 1) * NB)

        def gate_bank(s):
            return [6, 4, 6, 2][s]

        def y_units(s, i):
            return [MIX_UNITS, MIX_AT[1], FFN_AT[1]][s] - (2 if i == 0 else 0)

        def by_chunk(tile):
            return tile.rearrange("p (a c) k -> p a (c k)", a=HALF)

        def by_tile(hT, c0=0, nc_=KC):
            return hT[:, c0:c0 + nc_, :].rearrange("p c (t k) -> p t c k", t=TILES)

        def ada_rows(s):
            return w_ada[s // 2, s % 2].rearrange("(p k) n -> k p n", k=KC)

        def rows_of_g(layer, k):
            return norm_g[layer, k:k + 1, :].partition_broadcast(P)

        def job_reads(layer, j):
            return 15 * layer + (j + 1 if j < 9 else 9 + (j - 7) // 2)

        def merges(layer, j):
            return 6 * layer + (j - 8) // 2

        block = ctx.enter_context(nc.Block())

        @block.sync
        def _(sp):
            def load_unit(u, src):
                s, slot = raw_slot(u)
                ring = DEEP if u[0] >= FFN_AT[1] else RAW
                if not (isinstance(u[1], int) and isinstance(u[2], int) and place(u) < ring):
                    sp.wait_ge(lo_ready, place(u) - ring + 1)
                sp.dma_start(slot, src).then_inc(raw_landed[s], 16)

            def load_piece(p, s, part, c0):
                if not (isinstance(p[1], int) and p[0] + p[1] < ADA):
                    sp.wait_ge(ada_used, p[1] + (p[0] - ADA + 1))
                w = ada_rows(s)
                row = w[c0] if isinstance(c0, int) else w[bass.ds(c0, 1)].rearrange("o p n -> p (o n)")
                sp.dma_start(ada_piece[:, p[0] % ADA], row[:, part * D:(part + 1) * D]
                             ).then_inc(ada_landed[p[0] % ADA], 16)

            def load_bias(k, s, part):
                if k:
                    sp.wait_ge(bias_used, k)
                sp.dma_start(ada_bias[0:1, :], b_ada[s // 2, s % 2:s % 2 + 1, part * D:(part + 1) * D]
                             ).then_inc(bias_landed, 16)

            def load_g(s):
                sp.wait_ge(scale_ready, s + 1)
                if s < 3:
                    sp.dma_start(g_pre[:], rows_of_g((s + 1) // 2, 2 * ((s + 1) % 2))).then_inc(gpre_landed, 16)
                if s:
                    sp.wait_ge(gate_ready, s)
                sp.dma_start(g_post[:], rows_of_g(s // 2, 2 * (s % 2) + 1)).then_inc(gpost_landed, 16)

            def mixer(layer):
                p = 0
                for i in range(MIX_UNITS):
                    if i == RAW:
                        if layer:
                            sp.wait_ge(y_squared, 8)
                        else:
                            sp.wait_ge(start_used, 2 * KC)
                        sp.dma_start(wff[:], chunks(w_in[layer])[:, :, W_OFF["ff"]:W_OFF["ff"] + 8]
                                     ).then_inc(small_landed, 16)
                        sp.dma_start(f_bias[:], fox_f_bias[layer:layer + 1, :].partition_broadcast(P)
                                     ).then_inc(small_landed, 16)
                        sp.dma_start(dl[:], diff_lambda[layer:layer + 1].partition_broadcast(P)
                                     ).then_inc(small_landed, 16)
                        sp.dma_start(subln[:], diff_subln_g[layer:layer + 1, :].partition_broadcast(P)
                                     ).then_inc(small_landed, 16)
                    if i == RAW + 4:
                        load_g(2 * layer)
                    while p < MIX_PIECES and PIECE_AT[p] + PIECE_LEAD <= i:
                        s, part = ADA_MIX[layer][p // KC]
                        if p % KC == 0:
                            load_bias(BIAS0[2 * layer] + p // KC, s, part)
                        load_piece((PIECE0[2 * layer] + p, 0), s, part, p % KC)
                        p += 1
                    load_unit((MIX_AT[layer] + i, 0, 0), unit_source(layer, i))

            def ffn(u0, pas, w_gate, w_up, w_down, dense):
                def wide(at, step, w, cols):
                    for k in range(4):
                        load_unit((u0 + at + k, step, pas), chunks(w)[:, UC * k:UC * (k + 1), cols])

                def down(at, step, f):
                    rows = w_down.rearrange("(f r) n -> f r n", r=NB)
                    rows = rows[f] if isinstance(f, int) else rows[bass.ds(f, 1)].rearrange("o r n -> (o r) n")
                    for k in range(4):
                        load_unit((u0 + at + k, step, pas), chunks(rows)[
                            :, UC * (k % 2):UC * (k % 2 + 1), NB * (k // 2):NB * (k // 2 + 1)])

                wide(0, 0, w_gate, slice(0, NB))
                wide(4, 0, w_up, slice(0, NB))
                if dense:
                    load_g(1)
                    for part in range(2):
                        load_bias(BIAS0[1] + part, 2, part)
                        load_piece((PIECE0[1] + part, 0), 2, part, 0)
                with sp.Fori(1, FB) as f:
                    wide(8, f - 1, w_gate, bass.ds(f * NB, NB))
                    if dense:
                        for part in range(2):
                            load_piece((PIECE0[1] + 2 + part, (f - 1) * 2), 2, part, f)
                    wide(12, f - 1, w_up, bass.ds(f * NB, NB))
                    down(16, f - 1, f - 1)
                if dense:
                    for part in range(2):
                        load_piece((PIECE0[1] + 14 + part, 0), 2, part, KC - 1)
                down(PASS_UNITS - 4, 0, FB - 1)

            def expert(w, e):
                return w[0][bass.ds(e, 1)].rearrange("o k n -> (o k) n")

            sp.dma_start(c_col[:], c.rearrange("b (p k) -> p (b k)", p=P)).then_inc(c_landed, 16)
            for k in range(KC):
                sp.dma_start(ada_start[:, k], ada_rows(0)[k][:, 0:2 * D].rearrange(
                    "p (a n) -> p a n", a=2)).then_inc(start_landed[k], 16)
                if k < 2:
                    if k == 0:
                        sp.wait_ge(consts_ready, 1)
                    load_bias(k, 0, k)
            sp.dma_start(xs[:], x.rearrange("b (t p) d -> p (b t) d", p=P)).then_inc(x_landed, 16)
            sp.dma_start(g_pre[:], rows_of_g(0, 0)).then_inc(gpre_landed, 16)
            mixer(0)
            ffn(FFN_AT[0], 0, ffn_w_gate[0], ffn_w_up[0], ffn_w_down[0], True)
            mixer(1)
            sp.wait_ge(y_squared, 12)
            sp.dma_start(wr[:], chunks(moe_router[0])).then_inc(router_landed, 16)
            sp.wait_ge(gate_ready, 3)
            sp.dma_start(g_post[:], rows_of_g(1, 3)).then_inc(gpost_landed, 16)
            with sp.Fori(0, NE) as e:
                ffn(FFN_AT[1], e, expert(moe_w_gate, e), expert(moe_w_up, e), expert(moe_w_down, e), False)
            sp.wait_ge(passes_ready, 1)
            passes = sp.value_load(expert_i[0:1, MAX_OVER:MAX_OVER + 1], min_val=NE, max_val=NE + MAX_OVER)
            for j in range(MAX_OVER):
                with sp.If(passes > NE + j):
                    again = sp.value_load(expert_i[0:1, j:j + 1], min_val=0, max_val=NE - 1)
                    ffn(FFN_AT[1], NE + j, expert(moe_w_gate, again), expert(moe_w_up, again),
                        expert(moe_w_down, again), False)
            for t in range(TILES):
                sp.wait_ge(x_ready, 7 + t)
                sp.dma_start(out[0, t * P:(t + 1) * P, :], xs[:, t]).then_inc(stored, 16)
            sp.wait_ge(stored, 16 * TILES)

        @block.gpsimd
        def _(pool):
            own = Own(pool, pool_own)
            own(nc.gpsimd.memset(ada_bias[:], 0.0))
            own(nc.gpsimd.memset(ones[:], 1.0))
            own(nc.gpsimd.memset(eps_col[:], EPS))
            own(nc.gpsimd.memset(one_col[:], 1.0))
            own(nc.gpsimd.memset(ident[:], 0.0))
            own(nc.gpsimd.affine_select(out=ident[:], in_=ident[:], compare_op=ALU.not_equal, fill=1.0,
                                        base=0, pattern=[[-1, P]], channel_multiplier=1))
            own(nc.gpsimd.affine_select(out=tri[:], in_=ones[:], compare_op=ALU.is_ge, fill=0.0,
                                        base=0, pattern=[[1, P]], channel_multiplier=-1))
            nc.gpsimd.affine_select(out=tri_strict[:], in_=ones[:], compare_op=ALU.is_gt, fill=0.0,
                                    base=0, pattern=[[1, P]], channel_multiplier=-1).then_inc(consts_ready, 1)

            for layer in range(2):
                if layer:
                    pool.wait_ge(y_squared, 8)
                else:
                    pool.wait_ge(start_used, 2 * KC)
                own(nc.gpsimd.memset(zeros[:], 0.0))
                own(nc.gpsimd.memset(cum[:], 0.0))
                own(nc.gpsimd.memset(pick[:], 1.0))
                own(nc.gpsimd.affine_select(out=pick[:, 0:1], in_=pick[:, 0:1], compare_op=ALU.is_ge, fill=0.0,
                                            base=15, pattern=[[0, 1]], channel_multiplier=-1))
                own(nc.gpsimd.affine_select(out=pick[:, 1:2], in_=pick[:, 1:2], compare_op=ALU.is_ge, fill=0.0,
                                            base=-16, pattern=[[0, 1]], channel_multiplier=1))
                own(nc.gpsimd.affine_select(out=pick[:, 1:2], in_=pick[:, 1:2], compare_op=ALU.is_ge, fill=0.0,
                                            base=31, pattern=[[0, 1]], channel_multiplier=-1))
                for a in range(2):
                    own(nc.gpsimd.tensor_tensor(own_rows[:, a], ident[:, 16 * a:16 * a + 8],
                                                ident[:, 16 * a + 8:16 * a + 16], ALU.add))
                for m, op in enumerate((ALU.is_ge, ALU.is_gt)):
                    own(nc.gpsimd.affine_select(out=maskf[:, m * P:(m + 1) * P], in_=zeros[:, 0:P], compare_op=op,
                                                fill=MASKED, base=0, pattern=[[-1, P]], channel_multiplier=1))
                for b in range(TILES):
                    at = distf[:, b * P:(2 * b + 1) * P]
                    own(nc.gpsimd.iota(at, pattern=[[1, (b + 1) * P]], base=-b * P, channel_multiplier=-1,
                                       allow_small_or_imprecise_dtypes=True))
                    own(nc.gpsimd.affine_select(out=at, in_=at, compare_op=ALU.is_ge, fill=MASKED, base=b * P,
                                                pattern=[[-1, (b + 1) * P]], channel_multiplier=1))
                nc.gpsimd.memset(lam[:], 0.0).then_inc(mixconst_ready, 1)
                pool.wait_ge(t_read, NT * layer + T_AT[("cumT",)] + 1)
                own(nc.gpsimd.tensor_scalar(cum_mov[:], cumT[:], pick[:, 1:2], pick[:, 0:1], ALU.mult, ALU.add))
                for k in range(8):
                    if k >= 2:
                        pool.wait_ge(scores_done, NH * layer + k - 1)
                    nc.gpsimd.tensor_scalar(cum_sta[:, k % 2], cumT[:],
                                            own_rows[:, 0, k:k + 1], own_rows[:, 1, k:k + 1],
                                            ALU.mult, ALU.add).then_inc(cumsta_ready, 1)

            pool.wait_ge(y_squared, 12)
            own(nc.gpsimd.memset(table[:], 0.0))
            own(nc.gpsimd.memset(y_acc[:], 0.0))
            own(nc.gpsimd.memset(route[:], 0.0))
            own(nc.gpsimd.iota(slots[:], pattern=[[1, P]], base=0, channel_multiplier=0,
                               allow_small_or_imprecise_dtypes=True))
            own(nc.gpsimd.iota(rank[:], pattern=[[0, TILES], [-1, NE]], base=NE, channel_multiplier=0,
                               allow_small_or_imprecise_dtypes=True))
            nc.gpsimd.iota(index[:], pattern=[[1, NE]], base=0, channel_multiplier=0,
                           allow_small_or_imprecise_dtypes=True).then_inc(moeconst_ready, 1)

        @block.tensor
        def _(pe):
            mm = nc.tensor.matmul

            def unit(u, banks, stationary, c0, opens, closes):
                s = u[0] % SPLIT
                pe.wait_ge(lo_ready, place(u) + 1)
                for t, bank in enumerate(banks):
                    for k in range(UC):
                        hi, lo = stationary(t, c0 + k)
                        mm(bank, hi, w_hi[:, s, k], start=opens and k == 0, stop=False)
                        mm(bank, hi, w_lo[:, s, k], start=False, stop=False)
                        last = mm(bank, lo, w_hi[:, s, k], start=False, stop=closes and k == UC - 1)
                return last.then_inc(unit_used, 1)

            def of(hi, lo):
                return lambda t, c: (hi[:, c, t * P:(t + 1) * P], lo[:, c, t * P:(t + 1) * P])

            def narrow(o, t, w, chunks_=range(KC)):
                for k in chunks_:
                    for part, x in enumerate(of(hT_hi, hT_lo)(t, k)):
                        last = mm(o, x, w[:, k].rearrange("p a n -> p (a n)"), start=k == 0 and part == 0,
                                  stop=k == KC - 1 and part == 1)
                return last

            def bcast_sum(r, bank):
                for c in range(HALF):
                    last = mm(ps[:, bank + c], ones[:], ada_sum[:, r, c * NB:(c + 1) * NB], start=True, stop=True)
                last.then_inc(sums_bcast, 1)

            def gate(s):
                pe.wait_ge(ada_used, GATE_PIECES[s])
                if s in (0, 2):
                    pe.wait_ge(mT_ready, s + 2)
                bcast_sum(region(s, 2), gate_bank(s))

            def modulation(s):
                if s:
                    pe.wait_ge(ada_used, MOD_PIECES[s])
                    pe.wait_ge(gate_ready, s)
                bcast_sum(1, 6)
                bcast_sum(0, 4)

            def turn_rows(s, half):
                if half == 0:
                    pe.wait_ge(shift_ready, s + 1)
                else:
                    pe.wait_ge(scale_ready, s + 1)
                for t in range(TILES):
                    pe.wait_ge(h_ready, 4 * s + 2 * half + t + 1)
                    for k in range(4):
                        last = nc.tensor.transpose(ps[:, 4 + 2 * half + t, k * P:(k + 1) * P],
                                                   h[:, t, (4 * half + k) * P:(4 * half + k + 1) * P], ident[:])
                    last.then_inc(hT_filled, 1)

            def before_first(s, c0):
                if c0 == UC:
                    turn_rows(s, 1)
                if c0 in (0, 4):
                    pe.wait_ge(hT_ready, 2 * s + 1 + c0 // 4)

            def mixer(layer):
                heads0, uses0 = NH * layer, NT * layer

                def take_t(key):
                    if uses0 + T_AT[key]:
                        pe.wait_ge(t_read, uses0 + T_AT[key])

                def event(e):
                    what, key = e[1], e[1:]
                    if what == "ff":
                        take_t(key)
                        pe.wait_ge(wff_ready, layer + 1)
                        for t in range(TILES):
                            last = narrow(psT[:, 16 * t:16 * t + 16], t, wff_split)
                        last.then_inc(t_filled, 1)
                    elif what == "cum":
                        take_t(key)
                        pe.wait_ge(logf_ready, layer + 1)
                        mm(psT[:, 0:8], tri[:], fgate[:, 3, 0], start=True, stop=True)
                        mm(psT[:, 8:16], ones[:], fgate[:, 3, 0], start=True, stop=False)
                        mm(psT[:, 8:16], tri[:], fgate[:, 3, 1], start=False, stop=True).then_inc(t_filled, 1)
                    elif what == "cumT":
                        take_t(key)
                        pe.wait_ge(cumrows_ready, layer + 1)
                        for t in range(TILES):
                            last = nc.tensor.transpose(psT[:, t * P:(t + 1) * P], cum[:, t], ident[:])
                        last.then_inc(t_filled, 1)
                    elif what == "qkT":
                        _, _, n, qk, t = e
                        take_t(key)
                        pe.wait_ge(job_read, job_reads(layer, 3 * n + qk))
                        for k in range(4):
                            last = nc.tensor.transpose(psT[:, k * P:(k + 1) * P], staged[:, t, k * P:(k + 1) * P],
                                                       ident[:])
                        last.then_inc(t_filled, 1)
                    elif what == "scores":
                        scores(e[2])
                    elif what == "probsT":
                        k = e[2]
                        take_t(key)
                        if HEADS[k][0] == DIFF:
                            pe.wait_ge(comb_done, 4 * layer + k - 15)
                        else:
                            pe.wait_ge(exp_done, heads0 + k + 1)
                        buf = 0 if HEADS[k][0] == DIFF else k % 2
                        for b in range(3):
                            last = nc.tensor.transpose(psT[:, b * P:(b + 1) * P], probs[:, buf, b * P:(b + 1) * P],
                                                       ident[:])
                        last.then_inc(t_filled, 1)
                    elif what == "values":
                        values(e[2])
                    elif what == "oT":
                        _, _, n, t = e
                        take_t(key)
                        if n == DIFF:
                            pe.wait_ge(dscaled, layer + 1)
                        else:
                            pe.wait_ge(o_ready, heads0 + 8 * (n + 1))
                        for k in range(4):
                            last = nc.tensor.transpose(psT[:, k * P:(k + 1) * P],
                                                       o_rows[:, n % 2, t, k * P:(k + 1) * P], ident[:])
                        last.then_inc(t_filled, 1)
                    elif what == "gate":
                        gate(2 * layer)
                    elif what == "mergedT":
                        half = e[2]
                        pe.wait_ge(merged_ready, 6 * layer + 5 + half)
                        if half == 0:
                            pe.wait_ge(exp_done, heads0 + NH)
                        else:
                            pe.wait_ge(t_read, uses0 + NT)
                            pe.wait_ge(o_ready, heads0 + NH)
                        for t in range(TILES):
                            for k in range(4):
                                last = nc.tensor.transpose(
                                    ps[:, 4 + 2 * half + t, k * P:(k + 1) * P],
                                    h[:, t, half * NB + k * P:half * NB + (k + 1) * P], ident[:])
                        last.then_inc(mT_filled, 1)

                def scores(k):
                    branch, hd = HEADS[k]
                    n = branch % 2
                    maps = 2 if branch == DIFF else 1
                    if k >= 2:
                        last_user = k - 1 if branch == DIFF else k - 2
                        if HEADS[last_user][0] == SB:
                            pe.wait_ge(loga_ready, 8 * layer + last_user - 7)
                        else:
                            pe.wait_ge(exp_done, heads0 + last_user + 1)
                    if k in (0, 8, 16):
                        pe.wait_ge(t_read, uses0 + T_AT[("qkT", branch, 1, 1)] + 1)
                    if branch == FOX:
                        pe.wait_ge(cumsta_ready, 8 * layer + k + 1)
                        pe.wait_ge(mask_ready, layer + 1)
                    for m in range(maps):
                        bank = ps[:, 4 + (m if branch == DIFF else k % 2)]
                        for b in range(TILES):
                            keys = (b + 1) * P
                            o = bank[:, b * P:b * P + keys]
                            diag = bank[:, 2 * b * P:(2 * b + 1) * P]
                            if branch == FOX:
                                mm(o, cum_sta[:, k % 2, b * P:(b + 1) * P], cum_mov[:, 0:keys], start=True, stop=False,
                                   skip_group_check=True)
                                mm(diag, ident_r[:], mask_r[:, 0], start=False, stop=False, skip_group_check=True)
                            elif branch == SB:
                                mm(diag, ident_r[:], mask_r[:, 1], start=True, stop=False, skip_group_check=True)
                            else:
                                mm(o, slope_r[:, hd], dist_r[:, b * P:b * P + keys], start=True, stop=False,
                                   skip_group_check=True)
                            half = m if branch == DIFF else hd % 2
                            chunk = hd if branch == DIFF else hd // 2
                            rows = slice(half * HEAD, (half + 1) * HEAD)
                            last = mm(o, qkT[rows, n, 0, chunk, b * P:(b + 1) * P], qkT[rows, n, 1, chunk, 0:keys],
                                      start=False, stop=True, skip_group_check=True)
                    last.then_inc(scores_done, 1)

                def values(k):
                    branch, hd = HEADS[k]
                    n = branch % 2
                    pe.wait_ge(t_read, uses0 + T_AT[("probsT", k)] + 1)
                    if k:
                        pe.wait_ge(o_ready, heads0 + k)
                    if branch == FOX and k == 0:
                        pe.wait_ge(job_read, job_reads(layer, 2))
                    if branch == SB and k == 8:
                        pe.wait_ge(job_read, job_reads(layer, 5))
                    if branch == DIFF and k == 16:
                        pe.wait_ge(job_read, job_reads(layer, 8))
                    width, at = (P, (k % 2) * 2 * P) if branch == DIFF else (HEAD, (k % 4) * P)
                    for b in range(TILES):
                        o = psO[:, at + b * width:at + (b + 1) * width]
                        for s in range(b + 1):
                            last = mm(o, probsT[:, k % 2, (b + s) * P:(b + s + 1) * P],
                                      values_in[:, n, s, hd * width:(hd + 1) * width], start=s == 0, stop=s == b)
                    last.then_inc(values_done, 1)

                ev = list(EVENTS)
                for i, (j, c0, opens, closes) in enumerate(UNITS):
                    kind, n, col = JOBS[j]
                    if opens:
                        before = j - 2
                        if before >= 0:
                            if JOBS[before][0] == "br":
                                pe.wait_ge(merged_ready, merges(layer, before))
                            else:
                                pe.wait_ge(job_read, job_reads(layer, before))
                        if kind == "br":
                            pe.wait_ge(t_read, uses0 + T_AT[("oT", n, 1)] + 1)
                    if kind == "out" and opens:
                        pe.wait_ge(mT_ready, 2 * layer + 1)
                    if kind == "out" and c0 == 4:
                        pe.wait_ge(mT_ready, 2 * layer + 2)
                    sta = of(oT_hi, oT_lo) if kind == "br" else of(hT_hi, hT_lo)
                    b0 = pair(j)
                    if j == 0:
                        before_first(2 * layer, c0)
                    unit((MIX_AT[layer] + i, 0, 0), [ps[:, b0], ps[:, b0 + 1]], sta, c0, opens, closes)
                    while ev and ev[0][0] == i:
                        event(ev.pop(0))

            def ffn(u0, pas, g0, dense):
                tiles = range(TILES if dense else 1)
                gates = [ps[:, 4 + t] for t in tiles]
                ups = [ps[:, 6 + t] for t in tiles] if dense else [ps[:, 5]]
                downs = [[ps[:, 2 * c + t] for t in tiles] for c in range(HALF)] if dense else \
                    [[ps[:, c]] for c in range(HALF)]
                sta = of(hT_hi, hT_lo) if dense else of(xg_hi, xg_lo)
                act_sta = of(aT_hi, aT_lo)

                def steps(f):
                    return pas * FB + g0 + f

                def wide(at, step, banks):
                    for k in range(4):
                        if dense and at == 0:
                            before_first(1, UC * k)
                        unit((u0 + at + k, step, pas), banks, sta, UC * k, k == 0, k == 3)

                def down(at, step, closes=False):
                    for c in range(HALF):
                        for k in range(2):
                            unit((u0 + at + 2 * c + k, step, pas), downs[c], act_sta, UC * k, False,
                                 closes and k == 1)

                def turn(f):
                    pe.wait_ge(act_done, steps(f) + 1)
                    for t in tiles:
                        for k in range(4):
                            last = nc.tensor.transpose(ups[t][:, k * P:(k + 1) * P], act_s[:, t, k * P:(k + 1) * P],
                                                       ident[:])
                    last.then_inc(aT_filled, 1)

                wide(0, 0, gates)
                if not (isinstance(pas, int) and pas == 0 and g0 == 0):
                    pe.wait_ge(aT_ready, steps(0))
                wide(4, 0, ups)
                if not dense:
                    if not isinstance(pas, int):
                        scatter(pas)
                    for t in range(TILES):
                        last = nc.tensor.transpose(ps[:, 0, t * P:(t + 1) * P], pick_rows[:, t], ident[:])
                    last.then_inc(cols_filled, 1)
                turn(0)
                if not dense:
                    pe.wait_ge(cols_ready, pas + 1)
                for c in range(HALF):
                    for bank in downs[c]:
                        mm(bank, zero_r[:, 0:P], zero_r[:], start=True, stop=False)
                with pe.Fori(1, FB) as f:
                    wide(8, f - 1, gates)
                    pe.wait_ge(aT_ready, steps(f))
                    wide(12, f - 1, ups)
                    down(16, f - 1)
                    turn(f)
                if not dense:
                    gather(pas + 1)
                else:
                    gate(1)
                pe.wait_ge(aT_ready, steps(FB))
                down(PASS_UNITS - 4, 0, True)

            def gather(pas):
                pe.wait_ge(rows_picked, pas + 1)
                if not isinstance(pas, int):
                    pe.wait_ge(summed, pas * 2 - 2)
                for k in range(KC):
                    for t in range(TILES):
                        last = mm(ps[:, 6 + k // 4, (k % 4) * P:(k % 4 + 1) * P], h[:, t, k * P:(k + 1) * P],
                                  pick_rows[:, t], start=t == 0, stop=t == TILES - 1)
                last.then_inc(gathered, 1)

            def scatter(pas):
                pe.wait_ge(yexp_copied, pas)
                pe.wait_ge(cols_ready, pas)
                for t in range(TILES):
                    for c in range(HALF):
                        last = mm(ps[:, 2 + 4 * t + c], pick_cols[:, t * P:(t + 1) * P], y_exp[:, c * NB:(c + 1) * NB],
                                  start=True, stop=True)
                    last.then_inc(scattered[t], 1)

            pe.wait_ge(consts_ready, 1)
            pe.wait_ge(start_used, 2 * KC)
            modulation(0)
            turn_rows(0, 0)
            mixer(0)
            modulation(1)
            turn_rows(1, 0)
            ffn(FFN_AT[0], 0, 0, True)
            modulation(2)
            turn_rows(2, 0)
            mixer(1)
            modulation(3)
            turn_rows(3, 0)
            pe.wait_ge(wr_ready, 1)
            for half in range(2):
                if half:
                    turn_rows(3, 1)
                pe.wait_ge(hT_ready, 7 + half)
                for t in range(TILES):
                    last = narrow(ps[:, t, 0:2 * NE], t, wr_split, range(4 * half, 4 * half + 4))
            last.then_inc(router_done, 1)
            bcast_sum(region(3, 2), gate_bank(3))
            pe.wait_ge(sel_ready, 1)
            chosen = [route[:, 1, t] for t in range(TILES)]
            mm(ps[:, 1, 0:NE], tri_strict[:], chosen[0], start=True, stop=True)
            mm(ps[:, 1, NE:2 * NE], ones[:], chosen[0], start=True, stop=False)
            mm(ps[:, 1, NE:2 * NE], tri_strict[:], chosen[1], start=False, stop=True)
            mm(ps[:, 1, 2 * NE:3 * NE], ones[:], chosen[0], start=True, stop=False)
            mm(ps[:, 1, 2 * NE:3 * NE], ones[:], chosen[1], start=False, stop=True).then_inc(count_done, 1)
            gather(0)
            pe.wait_ge(count_read, 1)
            pe.wait_ge(xg_ready, 1)
            ffn(FFN_AT[1], 0, FB, False)
            pe.wait_ge(gate_ready, 4)
            pe.wait_ge(passes_ready, 1)
            passes = pe.value_load(expert_i[0:1, MAX_OVER:MAX_OVER + 1], min_val=NE, max_val=NE + MAX_OVER)
            with pe.Fori(1, passes) as pas:
                pe.wait_ge(xg_ready, pas + 1)
                ffn(FFN_AT[1], pas, FB, False)
            pe.wait_ge(xg_ready, passes + 1)
            scatter(passes)

        @block.scalar
        def _(act):
            own = Own(act, act_own)
            go = nc.scalar.activation

            def split(u):
                const, step, pas = u
                act.wait_ge(raw_landed[raw_slot(u)[0]], landings(u))
                if not (isinstance(step, int) and isinstance(pas, int) and place(u) < SPLIT):
                    act.wait_ge(unit_used, place(u) - SPLIT + 1)
                go(w_hi[:, const % SPLIT], raw_slot(u)[1], ACT.Copy).then_inc(hi_ready, 1)

            done = [0]

            def split_to(n):
                while done[0] < n:
                    split((done[0], 0, 0))
                    done[0] += 1

            def use_silu():
                nc.scalar.preload_act_table_set("silu_and_others")

            def use_exp_ln():
                nc.scalar.preload_act_table_set("natural_log_exp_and_others")

            def close(s):
                if s < 3:
                    junk = gate_s if s == 1 else staged
                    for i in range(HALF):
                        act.wait_ge(unit_used, y_units(s, i))
                        for t in range(TILES):
                            if t:
                                act.wait_ge(y_scaled, 4 * s + 2 * i + 1)
                            go(junk[:, t] if i else half_rows(mod_junk)[:, t], y_block(s, i, t)[0], ACT.Square,
                               accum_out=stat[:, 2 * i + t:2 * i + t + 1]).then_inc(y_squared, 1)
                else:
                    for t in range(TILES):
                        go(gate_s.rearrange("p a n -> p (a n)"), y_acc[:, t], ACT.Square,
                           accum_out=stat[:, 4 + t:5 + t]).then_inc(y_squared, 1)
                        act.wait_ge(y_squared, 4 * s + t + 1)
                if s < 3:
                    act.wait_ge(y_summed, s + 1)
                own(go(stat[:, 6:8], stat[:, 4:6], ACT.Ln, bias=eps_col[:, 0:1], scale=1.0 / D))
                go(stat[:, 8:10], stat[:, 6:8], ACT.Exp, scale=-0.5).then_inc(rstd_ready, 2)
                if s < 3:
                    shift(s + 1)

            def shift(s):
                act.wait_ge(sums_bcast, 2 + 3 * s)
                go(half_rows(mod_shift), ps[:, 4:6], ACT.Copy).then_inc(shift_ready, 1)

            def norm(s):
                for t in range(TILES):
                    if s:
                        act.wait_ge(x_ready, 2 * (s - 1) + t + 1)
                    elif t == 0:
                        act.wait_ge(x_landed, 16)
                    own(go(mod_junk[:], xs[:, t], ACT.Square, accum_out=stat[:, 10 + t:11 + t]))
                    own(go(stat[:, 12 + t:13 + t], stat[:, 10 + t:11 + t], ACT.Ln, bias=eps_col[:, 0:1],
                           scale=1.0 / D))
                    go(stat[:, 14 + t:15 + t], stat[:, 12 + t:13 + t], ACT.Exp, scale=-0.5).then_inc(rstd_ready, 1)
                if s == 0:
                    shift(0)
                    split_to(AHEAD)
                elif s == 3:
                    act.wait_ge(router_landed, 16)
                    go(wr_split[:, :, 0], wr[:], ACT.Copy).then_inc(wr_half, 1)
                for half in range(2):
                    for t in range(TILES):
                        act.wait_ge(hT_filled, 4 * s + 2 * half + t + 1)
                        go(by_tile(hT_hi, 4 * half, 4)[:, t],
                           ps[:, 4 + 2 * half + t].rearrange("p (c k) -> p c k", k=P), ACT.Copy
                           ).then_inc(hT_half, 1)

            def mixer(layer):
                heads0, uses0 = NH * layer, NT * layer
                base = MIX_AT[layer]

                def job_wait(j):
                    act.wait_ge(unit_used, base + JOB_END[j] + 1)

                def event(e):
                    what = e[1]
                    if what == "wff":
                        act.wait_ge(small_landed, 64 * (layer + 1))
                        go(wff_split[:, :, 0], wff[:], ACT.Copy).then_inc(wff_half, 1)
                    elif what == "consts":
                        act.wait_ge(mixconst_ready, layer + 1)
                        for b in range(4):
                            go(slope_r[:, b], ident[:], ACT.Copy, scale=2.0 ** (-2 * (b + 1)))
                        go(dist_r[:], distf[:], ACT.Copy)
                        go(mask_r[:], maskf.rearrange("p (m k) -> p m k", m=2), ACT.Copy).then_inc(mask_ready, 1)
                    elif what == "logf":
                        act.wait_ge(fpre_ready, layer + 1)
                        own(go(fgate[:, 1], fgate[:, 0], ACT.Abs))
                        own(go(fgate[:, 1], fgate[:, 1], ACT.Exp, scale=-1.0))
                        go(fgate[:, 2], fgate[:, 1], ACT.Ln, bias=one_col[:, 0:1]).then_inc(fsoft_ready, 1)
                    elif what == "lam":
                        act.wait_ge(lam_a, layer + 1)
                        go(lam[:, 2:4], lam[:, 0:2], ACT.Exp).then_inc(lam_b, 1)
                    elif what == "cumT":
                        act.wait_ge(t_filled, uses0 + T_AT[e[1:]] + 1)
                        go(cumT[:], psT[:, 0:SEQ], ACT.Copy).then_inc(t_read, 1)
                    elif what == "evac":
                        j = e[2]
                        kind, n, _ = JOBS[j]
                        job_wait(j)
                        src = ps[:, pair(j):pair(j) + 2]
                        if kind == "v":
                            go(values_in[:, n % 2], src, ACT.Copy).then_inc(job_read, 1)
                        else:
                            go(staged[:], src, ACT.Copy, scale=HEAD ** -0.5 if kind == "q" else 1.0
                               ).then_inc(job_read, 1)
                    elif what == "qkT":
                        _, _, n, qk, t = e
                        act.wait_ge(t_filled, uses0 + T_AT[e[1:]] + 1)
                        go(qkT[:, n % 2, qk, :, t * P:(t + 1) * P], psT.rearrange("p (c k) -> p c k", k=P),
                           ACT.Copy).then_inc(t_read, 1)
                    elif what == "scores" and HEADS[e[2]][0] == SB:
                        k = e[2]
                        act.wait_ge(scores_done, heads0 + k + 1)
                        z = ps[:, 4 + k % 2, 0:3 * P]
                        s = soft[:, k % 2]
                        own(go(s, z, ACT.Abs))
                        own(go(s, s, ACT.Exp, scale=-1.0))
                        go(s, s, ACT.Ln, bias=one_col[:, 0:1]).then_inc(soft_ready, 1)
                    elif what == "exp":
                        k = e[2]
                        branch = HEADS[k][0]
                        before = k - 1 if branch == DIFF else k - 2
                        if before >= 0:
                            act.wait_ge(t_filled, uses0 + T_AT[("probsT", before)] + 1)
                        if branch == SB:
                            act.wait_ge(loga_ready, 8 * layer + k - 7)
                            go(probs[:, k % 2], soft[:, k % 2], ACT.Exp).then_inc(exp_done, 1)
                            return
                        act.wait_ge(max_ready, 12 * layer + (k + 1 if branch == FOX else k - 7))
                        for m in range(2 if branch == DIFF else 1):
                            bank, buf = (4 + m, m) if branch == DIFF else (4 + k % 2, k % 2)
                            for b in range(TILES):
                                at = slice(b * P, b * P + (b + 1) * P)
                                col = 2 * m + b
                                last = go(probs[:, buf, at], ps[:, bank, at], ACT.Exp,
                                          bias=hstat[:, k % 4, col:col + 1],
                                          accum_out=hstat[:, k % 4, 4 + col:5 + col])
                        last.then_inc(exp_done, 1)
                    elif what == "probsT":
                        k = e[2]
                        act.wait_ge(t_filled, uses0 + T_AT[e[1:]] + 1)
                        go(probsT[:, k % 2], psT[:, 0:3 * P], ACT.Copy).then_inc(t_read, 1)
                    elif what == "oT":
                        _, _, n, t = e
                        act.wait_ge(t_filled, uses0 + T_AT[e[1:]] + 1)
                        go(by_tile(oT_hi, 0, 4)[:, t], psT.rearrange("p (c k) -> p c k", k=P), ACT.Copy
                           ).then_inc(t_half, 1)
                    elif what == "diffscale":
                        act.wait_ge(dsum_ready, layer + 1)
                        own(go(dstat[:, 1], dstat[:, 0], ACT.Ln, bias=eps_col[:, 0:1], scale=1.0 / P))
                        go(dstat[:, 1], dstat[:, 1], ACT.Exp, scale=-0.5).then_inc(drstd_ready, 1)
                    elif what == "gates":
                        _, _, n, col = e
                        j = 9 + 4 * n + 2 * col
                        job_wait(j)
                        if n or col:
                            act.wait_ge(merged_ready, 6 * layer + 2 * n + col)
                        go(staged[:], ps[:, pair(j):pair(j) + 2], ACT.Sigmoid).then_inc(job_read, 1)
                    elif what == "mergedT":
                        half = e[2]
                        act.wait_ge(mT_filled, 2 * layer + half + 1)
                        dst = by_tile(hT_hi, 4 * half, 4)
                        for t in range(TILES):
                            last = go(dst[:, t], ps[:, 4 + 2 * half + t].rearrange("p (c k) -> p c k", k=P), ACT.Copy)
                        last.then_inc(mT_half, 1)

                limit = base + MIX_UNITS + (AHEAD if layer == 0 else 0)
                for e in EVENTS:
                    split_to(min(base + e[0] + 1 + AHEAD, limit))
                    event(e)
                split_to(limit)

            def ffn(u0, pas, g0, dense):
                n = TILES if dense else 1
                gates = ps[:, 4:4 + n]
                ups = ps[:, 6:8] if dense else ps[:, 5:6]

                def steps(f):
                    return pas * FB + g0 + f

                def silu(f, at, step):
                    act.wait_ge(unit_used, place((u0 + at, step, pas)))
                    if not (isinstance(f, int) and dense):
                        act.wait_ge(act_done, steps(f))
                    go(gate_s[:, 0:n], gates, ACT.Silu).then_inc(silu_done, 1)

                def turned(f):
                    act.wait_ge(aT_filled, steps(f) + 1)
                    for t in range(n):
                        last = go(by_tile(aT_hi, 0, 4)[:, t], ups[:, t].rearrange("p (c k) -> p c k", k=P), ACT.Copy)
                    last.then_inc(aT_half, 1)

                def splits(at, step, k):
                    for i in range(k):
                        split((u0 + at + i, step, pas))

                if not dense:
                    if not isinstance(pas, int):
                        splits(0, 0, AHEAD)
                        act.wait_ge(unit_used, place((u0, 0, pas)))
                        go(half_rows(y_exp), ps[:, 0:2], ACT.Copy).then_inc(yexp_copied, 1)
                splits(3, 0, 4)
                silu(0, 4, 0)
                splits(7, 0, 4)
                if not dense:
                    act.wait_ge(cols_filled, pas + 1)
                    go(pick_cols[:], ps[:, 0, 0:SEQ], ACT.Copy).then_inc(cols_ready, 1)
                turned(0)
                with act.Fori(1, FB) as f:
                    splits(11, f - 1, 4)
                    silu(f, 12, f - 1)
                    splits(15, f - 1, 8)
                    turned(f)
                splits(PASS_UNITS - 1, 0, 1)
                if not dense:
                    act.wait_ge(gathered, pas + 2)
                    go(by_chunk(xg_hi), ps[:, 6:8], ACT.Copy).then_inc(xg_half, 1)

            act.wait_ge(c_landed, 16)
            go(c_silu[:], c_col[:], ACT.Silu).then_inc(c_ready, 1)
            act.wait_ge(consts_ready, 1)
            go(ident_r[:], ident[:], ACT.Copy)
            use_exp_ln()
            norm(0)
            mixer(0)
            use_exp_ln()
            close(0)
            norm(1)
            ffn(FFN_AT[0], 0, 0, True)
            done[0] = FFN_AT[0] + PASS_UNITS
            use_exp_ln()
            split_to(MIX_AT[1] + 2)
            close(1)
            norm(2)
            mixer(1)
            use_exp_ln()
            close(2)
            norm(3)
            for k in range(AHEAD):
                split((FFN_AT[1] + k, 0, 0))
            act.wait_ge(wdiff_ready, 1)
            go(rs[:, 5], rs[:, 4], ACT.Exp).then_inc(wexp_ready, 1)
            use_silu()
            act.wait_ge(gathered, 1)
            go(by_chunk(xg_hi), ps[:, 6:8], ACT.Copy).then_inc(xg_half, 1)
            ffn(FFN_AT[1], 0, FB, False)
            act.wait_ge(passes_ready, 1)
            passes = act.value_load(expert_i[0:1, MAX_OVER:MAX_OVER + 1], min_val=NE, max_val=NE + MAX_OVER)
            with act.Fori(1, passes) as pas:
                ffn(FFN_AT[1], pas, FB, False)
            use_exp_ln()
            act.wait_ge(unit_used, passes * PASS_UNITS + FFN_AT[1])
            go(half_rows(y_exp), ps[:, 0:2], ACT.Copy).then_inc(yexp_copied, 1)
            act.wait_ge(summed, passes * 2)
            close(3)

        @block.vector
        def _(dve):
            own = Own(dve, dve_own)
            tt, ts, stt = nc.vector.tensor_tensor, nc.vector.tensor_scalar, nc.vector.scalar_tensor_tensor
            copy = nc.vector.tensor_copy
            reduce = nc.vector.tensor_reduce

            def split(u):
                dve.wait_ge(hi_ready, place(u) + 1)
                tt(w_lo[:, u[0] % SPLIT], raw_slot(u)[1], w_hi[:, u[0] % SPLIT].bitcast(F32), ALU.subtract
                   ).then_inc(lo_ready, 1)

            done = [0]

            def split_to(n):
                while done[0] < n:
                    split((done[0], 0, 0))
                    done[0] += 1

            def piece(p, s, part, c0, bias=None):
                dve.wait_ge(ada_landed[p[0] % ADA], p[1] * (16 // ADA) + 16 * (p[0] // ADA + 1))
                if not (isinstance(p[1], int) and p[0] == 0):
                    dve.wait_ge(ada_used, p[1] + p[0])
                total = ada_sum[:, region(s, part)]
                if bias is not None:
                    dve.wait_ge(bias_landed, 16 * (bias + 1))
                w = ada_piece[:, p[0] % ADA]
                col = c_silu[:, c0:c0 + 1] if isinstance(c0, int) else c_cur[:, 0:1]
                ins = stt(total, w, col, total if bias is None else ada_bias[:], ALU.mult, ALU.add)
                ins.then_inc(ada_used, 1)
                if bias is not None:
                    dve.wait_ge(ada_used, p[0] + 1)
                    dve.sem_inc(bias_used, 1)

            def gate(s):
                bank = gate_bank(s)
                dve.wait_ge(sums_bcast, 3 + 3 * s)
                dve.wait_ge(gpost_landed, 16 * (s + 1))
                tt(half_rows(mod_gate), ps[:, bank:bank + 2], half_rows(g_post), ALU.mult).then_inc(gate_ready, 1)

            def scale(s):
                dve.wait_ge(sums_bcast, 1 + 3 * s)
                dve.wait_ge(gpre_landed, 16 * (s + 1))
                stt(half_rows(mod_scale), ps[:, 6:8], 1.0, half_rows(g_pre), ALU.add, ALU.mult).then_inc(scale_ready, 1)

            def close(s):
                dve.wait_ge(gate_ready, s + 1)
                if s < 3:
                    for i in range(HALF):
                        dve.wait_ge(unit_used, y_units(s, i))
                        for t in (1, 0):
                            if t == 0:
                                dve.wait_ge(y_squared, 4 * s + 2 * i + 1)
                            y, cols = y_block(s, i, t)
                            tt(h[:, t, cols], y, mod_gate[:, cols], ALU.mult).then_inc(y_scaled, 1)
                    dve.wait_ge(y_squared, 4 * s + 4)
                    tt(stat[:, 4:6], stat[:, 0:2], stat[:, 2:4], ALU.add).then_inc(y_summed, 1)
                    scale(s + 1)
                    dve.wait_ge(y_scaled, 4 * s + 4)
                else:
                    for t in range(TILES):
                        own(tt(h[:, t], y_acc[:, t], mod_gate[:], ALU.mult))
                dve.wait_ge(rstd_ready, 4 + 4 * s)
                for t in range(TILES):
                    stt(xs[:, t], h[:, t], stat[:, 8 + t:9 + t], xs[:, t], ALU.mult, ALU.add).then_inc(x_ready, 1)

            def norm(s):
                dve.wait_ge(scale_ready, s + 1)
                if s:
                    dve.wait_ge(x_ready, 2 * s)
                def modulate(half, t):
                    cols = slice(half * NB, (half + 1) * NB)
                    if half == 0:
                        dve.wait_ge(rstd_ready, 4 * s + t + 1)
                    own(stt(h[:, t, cols], xs[:, t, cols], stat[:, 14 + t:15 + t], mod_scale[:, cols],
                            ALU.mult, ALU.mult))
                    if half == 0 and t == 0:
                        dve.wait_ge(shift_ready, s + 1)
                    tt(h[:, t, cols], h[:, t, cols], mod_shift[:, cols], ALU.add).then_inc(h_ready, 1)

                def low(half, t):
                    dve.wait_ge(hT_half, 4 * s + 2 * half + t + 1)
                    return tt(by_tile(hT_lo, 4 * half, 4)[:, t],
                              ps[:, 4 + 2 * half + t].rearrange("p (c k) -> p c k", k=P),
                              by_tile(hT_hi, 4 * half, 4)[:, t].bitcast(F32), ALU.subtract)

                modulate(0, 0)
                modulate(0, 1)
                modulate(1, 0)
                if s == 3:
                    dve.wait_ge(wr_half, 1)
                    tt(wr_split[:, :, 1], wr[:], wr_split[:, :, 0].bitcast(F32), ALU.subtract).then_inc(wr_ready, 1)
                low(0, 0)
                low(0, 1).then_inc(hT_ready, 1)
                if s == 0:
                    split_to(2)
                modulate(1, 1)
                low(1, 0)
                low(1, 1).then_inc(hT_ready, 1)

            def mixer(layer):
                heads0, uses0 = NH * layer, NT * layer
                base = MIX_AT[layer]

                def event(e):
                    what = e[1]
                    if what == "wff":
                        dve.wait_ge(wff_half, layer + 1)
                        tt(wff_split[:, :, 1], wff[:], wff_split[:, :, 0].bitcast(F32), ALU.subtract
                           ).then_inc(wff_ready, 1)
                    elif what == "ff":
                        dve.wait_ge(t_filled, uses0 + T_AT[e[1:]] + 1)
                        pre = psT[:, 0:32].rearrange("p (t a n) -> p a t n", t=TILES, a=2)
                        own(tt(fgate[:, 0], pre[:, 0], f_bias[:].unsqueeze(1).to_broadcast([P, TILES, 8]), ALU.add))
                        tt(fgate[:, 0], fgate[:, 0], pre[:, 1], ALU.add).then_inc(fpre_ready, 1)
                        dve.wait_ge(fpre_ready, layer + 1)
                        dve.sem_inc(t_read, 1)
                    elif what == "lam":
                        own(tt(tail[:, 0:P].rearrange("p (a n) -> p a n", a=2), dl[:, 0::2], dl[:, 1::2], ALU.mult))
                        dve.wait_ge(mixconst_ready, layer + 1)
                        reduce(lam[:, 0:2], tail[:, 0:P].rearrange("p (a n) -> p a n", a=2), AX.X, ALU.add
                               ).then_inc(lam_a, 1)
                        dve.wait_ge(fsoft_ready, layer + 1)
                        stt(fgate[:, 3], fgate[:, 0], 0.0, fgate[:, 2], ALU.min, ALU.subtract).then_inc(logf_ready, 1)
                    elif what == "cum":
                        dve.wait_ge(t_filled, uses0 + T_AT[e[1:]] + 1)
                        src = psT[:, 0:16].rearrange("p (t n) -> p t n", t=TILES)
                        own(copy(cum_split[:, :, 0:8], src))
                        own(tt(cum_split[:, :, 8:16], src, cum_split[:, :, 0:8].bitcast(F32), ALU.subtract))
                        copy(cum[:, :, 0:16], cum_split[:].bitcast(F32))
                        own(ts(cum[:, :, 16:32], cum_split[:].bitcast(F32), -1.0, None, ALU.mult))
                        dve.sem_inc(cumrows_ready, 1)
                        dve.sem_inc(t_read, 1)
                    elif what == "lam2":
                        dve.wait_ge(lam_b, layer + 1)
                        own(tt(lam[:, 4:5], lam[:, 3:4], lam[:, 2:3], ALU.subtract))
                        own(ts(lam[:, 5:6], lam[:, 4:5], -lam_init[layer], None, ALU.add))
                        own(ts(subln[:], subln[:], 1.0 - lam_init[layer], None, ALU.mult))
                    elif what == "scores":
                        k = e[2]
                        branch = HEADS[k][0]
                        if branch == SB:
                            dve.wait_ge(soft_ready, 8 * layer + k - 7)
                            z = ps[:, 4 + k % 2, 0:3 * P]
                            own(stt(stay[:], z, 0.0, soft[:, k % 2], ALU.max, ALU.add))
                            for b in range(TILES):
                                at = slice(b * P, b * P + (b + 1) * P)
                                last = nc.vector.tensor_tensor_scan(tail[:, at][:, ::-1], stay[:, at][:, ::-1],
                                                                    zeros[:, 0:(b + 1) * P], 0.0, ALU.add, ALU.add)
                            own(last)
                            tt(soft[:, k % 2], z, tail[:], ALU.subtract).then_inc(loga_ready, 1)
                            return
                        dve.wait_ge(scores_done, heads0 + k + 1)
                        for b in range(TILES):
                            at = slice(b * P, b * P + (b + 1) * P)
                            if branch == DIFF:
                                last = reduce(hstat[:, k % 4, b:4:2], ps[:, 4:6, at], AX.X, ALU.max, negate=True)
                            else:
                                last = reduce(hstat[:, k % 4, b:b + 1], ps[:, 4 + k % 2, at], AX.X, ALU.max, negate=True)
                        last.then_inc(max_ready, 1)
                    elif what == "combine":
                        k = e[2]
                        s = hstat[:, k % 4]
                        dve.wait_ge(exp_done, heads0 + k + 1)
                        own(nc.vector.reciprocal(s[:, 8:12], s[:, 4:8]))
                        own(ts(s[:, 10:12], s[:, 10:12], lam[:, 5:6], None, ALU.mult))
                        for b in range(TILES):
                            at = slice(b * P, b * P + (b + 1) * P)
                            last = ts(probs[:, 1, at], probs[:, 1, at], s[:, 10 + b:11 + b], None, ALU.mult)
                        own(last)
                        for b in range(TILES):
                            at = slice(b * P, b * P + (b + 1) * P)
                            last = stt(probs[:, 0, at], probs[:, 0, at], s[:, 8 + b:9 + b], probs[:, 1, at],
                                       ALU.mult, ALU.add)
                        last.then_inc(comb_done, 1)
                    elif what == "values":
                        k = e[2]
                        branch, hd = HEADS[k]
                        width, at = (P, (k % 2) * 2 * P) if branch == DIFF else (HEAD, (k % 4) * P)
                        src = psO[:, at:at + 2 * width].rearrange("p (t n) -> p t n", t=TILES)
                        dst = o_rows[:, branch % 2, :, hd * width:(hd + 1) * width]
                        if branch == FOX:
                            s = hstat[:, k % 4]
                            dve.wait_ge(exp_done, heads0 + k + 1)
                            own(nc.vector.reciprocal(s[:, 8:10], s[:, 4:6]))
                            dve.wait_ge(values_done, heads0 + k + 1)
                            tt(dst, src, s[:, 8:10].unsqueeze(2).to_broadcast([P, TILES, HEAD]), ALU.mult
                               ).then_inc(o_ready, 1)
                        else:
                            dve.wait_ge(values_done, heads0 + k + 1)
                            copy(dst, src).then_inc(o_ready, 1)
                    elif what == "diffnorm":
                        dve.wait_ge(o_ready, heads0 + NH)
                        own(tt(values_in[:, 1], o_rows[:, 0], o_rows[:, 0], ALU.mult))
                        reduce(dstat[:, 0], values_in[:, 1].rearrange("p t (n k) -> p (t n) k", k=P), AX.X, ALU.add
                               ).then_inc(dsum_ready, 1)
                    elif what == "diffscale":
                        dve.wait_ge(drstd_ready, layer + 1)
                        o = o_rows[:, 0].rearrange("p t (n k) -> p (t n) k", k=P)
                        own(tt(o, o, dstat[:, 1].unsqueeze(2).to_broadcast([P, 8, P]), ALU.mult))
                        tt(o, o, subln[:].unsqueeze(1).to_broadcast([P, 8, P]), ALU.mult).then_inc(dscaled, 1)
                    elif what == "oT":
                        _, _, n, t = e
                        dve.wait_ge(t_half, 6 * layer + 2 * n + t + 1)
                        tt(by_tile(oT_lo, 0, 4)[:, t], psT.rearrange("p (c k) -> p c k", k=P),
                           by_tile(oT_hi, 0, 4)[:, t].bitcast(F32), ALU.subtract).then_inc(t_read, 1)
                    elif what == "merge":
                        _, _, n, col = e
                        j = 9 + 4 * n + 2 * col + 1
                        dve.wait_ge(job_read, job_reads(layer, j - 1))
                        dve.wait_ge(unit_used, base + JOB_END[j] + 1)
                        br = ps[:, pair(j):pair(j) + 2]
                        dst = h[:, :, col * NB:(col + 1) * NB]
                        if n == 0:
                            tt(dst, br, staged[:], ALU.mult).then_inc(merged_ready, 1)
                        else:
                            own(tt(staged[:], br, staged[:], ALU.mult))
                            tt(dst, dst, staged[:], ALU.add).then_inc(merged_ready, 1)
                    elif what == "gate":
                        gate(2 * layer)
                    elif what == "mergedT":
                        half = e[2]
                        dve.wait_ge(mT_half, 2 * layer + half + 1)
                        for t in range(TILES):
                            last = tt(by_tile(hT_lo, 4 * half, 4)[:, t],
                                      ps[:, 4 + 2 * half + t].rearrange("p (c k) -> p c k", k=P),
                                      by_tile(hT_hi, 4 * half, 4)[:, t].bitcast(F32), ALU.subtract)
                        last.then_inc(mT_ready, 1)

                limit = base + MIX_UNITS + (AHEAD if layer == 0 else 0)
                p = 0
                for i in range(MIX_UNITS):
                    split_to(min(base + i + 1 + AHEAD, limit))
                    for e in EVENTS:
                        if e[0] == i:
                            event(e)
                    while p < MIX_PIECES and PIECE_AT[p] <= i:
                        s, part = ADA_MIX[layer][p // KC]
                        piece((PIECE0[2 * layer] + p, 0), s, part, p % KC,
                              BIAS0[2 * layer] + p // KC if p % KC == 0 else None)
                        p += 1

            def ffn(u0, pas, g0, dense):
                n = TILES if dense else 1
                ups = ps[:, 6:8] if dense else ps[:, 5:6]

                def steps(f):
                    return pas * FB + g0 + f

                def splits(at, step, k):
                    for i in range(k):
                        split((u0 + at + i, step, pas))

                def product(f, at, step):
                    dve.wait_ge(silu_done, steps(f) + 1)
                    dve.wait_ge(unit_used, place((u0 + at, step, pas)))
                    tt(act_s[:, 0:n], gate_s[:, 0:n], ups, ALU.mult).then_inc(act_done, 1)

                def turned(f):
                    dve.wait_ge(aT_half, steps(f) + 1)
                    for t in range(n):
                        last = tt(by_tile(aT_lo, 0, 4)[:, t], ups[:, t].rearrange("p (c k) -> p c k", k=P),
                                  by_tile(aT_hi, 0, 4)[:, t].bitcast(F32), ALU.subtract)
                    last.then_inc(aT_ready, 1)

                if not dense and not isinstance(pas, int):
                    splits(0, 0, AHEAD)
                splits(3, 0, 4)
                if dense:
                    for part in range(2):
                        piece((PIECE0[1] + part, 0), 2, part, 0, BIAS0[1] + part)
                splits(7, 0, 4)
                product(0, 8, 0)
                if not dense and not isinstance(pas, int):
                    gather_sum(pas)
                turned(0)
                if not dense:
                    pick(pas + 1)
                with dve.Fori(1, FB) as f:
                    splits(11, f - 1, 4)
                    if dense:
                        copy(c_cur[:], c_silu[:, bass.ds(f, 1)]).then_inc(ccur_ready, 1)
                        dve.wait_ge(ccur_ready, f)
                        for part in range(2):
                            piece((PIECE0[1] + 2 + part, (f - 1) * 2), 2, part, f)
                    splits(15, f - 1, 4)
                    product(f, 16, f - 1)
                    splits(19, f - 1, 4)
                    turned(f)
                splits(PASS_UNITS - 1, 0, 1)
                if dense:
                    gate(1)
                    for part in range(2):
                        piece((PIECE0[1] + 14 + part, 0), 2, part, KC - 1)
                else:
                    dve.wait_ge(xg_half, pas + 2)
                    gathered_low()

            def gathered_low():
                tt(by_chunk(xg_lo), ps[:, 6:8], by_chunk(xg_hi).bitcast(F32), ALU.subtract).then_inc(xg_ready, 1)

            def gather_sum(pas):
                at = table[:, bass.ds(pas, 1)] if not isinstance(pas, int) else table[:, pas:pas + 1]
                copy(cur_w[:], at.rearrange("p o q t -> p (o q) t")[:, 2]).then_inc(curw_ready, 1)
                dve.wait_ge(curw_ready, pas)
                for t in range(TILES):
                    dve.wait_ge(scattered[t], pas)
                    dst = half_rows(y_acc[:, t])
                    stt(dst, ps[:, 2 + 4 * t:4 + 4 * t], cur_w[:, t:t + 1], dst, ALU.mult, ALU.add).then_inc(summed, 1)

            def pick(pas):
                at = table[:, bass.ds(pas + 1, 1)] if not isinstance(pas, int) else table[:, pas + 1:pas + 2]
                if not (isinstance(pas, int) and pas == 0):
                    dve.wait_ge(cols_filled, pas)
                copy(cur[:], at.rearrange("p o q t -> p (o q) t")).then_inc(cur_ready, 1)
                dve.wait_ge(cur_ready, pas + 1)
                for t in range(TILES):
                    last = ts(pick_rows[:, t], slots[:], cur[:, 0, t:t + 1], cur[:, 1, t:t + 1], ALU.is_equal, ALU.mult)
                last.then_inc(rows_picked, 1)

            def routing():
                bc = lambda col: col.unsqueeze(2).to_broadcast([P, TILES, NE])
                both = ps[:, 0:TILES, 0:2 * NE].rearrange("p t (a e) -> p a t e", a=2)
                own(copy(rt[:, 0], both[:, 0]))
                own(tt(rt[:, 0], rt[:, 0], both[:, 1], ALU.add))
                for a in range(2):
                    logits, equal, first, hot = rt[:, 5 * a], rt[:, 5 * a + 1], rt[:, 5 * a + 2], rt[:, 5 * a + 3]
                    own(reduce(rs[:, 2 * a], logits, AX.X, ALU.max))
                    own(tt(equal, logits, bc(rs[:, 2 * a]), ALU.is_equal))
                    own(tt(first, equal, rank[:], ALU.mult))
                    own(reduce(rs[:, 2 * a + 1], first, AX.X, ALU.max))
                    own(tt(hot, first, bc(rs[:, 2 * a + 1]), ALU.is_equal))
                    if a == 0:
                        own(stt(rt[:, 5], hot, FAR, logits, ALU.mult, ALU.add))
                tt(rs[:, 4], rs[:, 2], rs[:, 0], ALU.subtract).then_inc(wdiff_ready, 1)
                tt(route[:, 1], rt[:, 3], rt[:, 8], ALU.add).then_inc(sel_ready, 1)
                dve.wait_ge(wexp_ready, 1)
                own(ts(rs[:, 6], rs[:, 5], 1.0, None, ALU.add))
                own(nc.vector.reciprocal(rs[:, 7], rs[:, 6]))
                own(tt(rs[:, 8], rs[:, 5], rs[:, 7], ALU.mult))
                tt(rt[:, 4], rt[:, 3], bc(rs[:, 7]), ALU.mult)
                own(tt(rt[:, 9], rt[:, 8], bc(rs[:, 8]), ALU.mult))
                tt(route[:, 2], rt[:, 4], rt[:, 9], ALU.add)
                dve.wait_ge(count_done, 1)
                copy(route[:, 0], ps[:, 1, 0:2 * NE].rearrange("p (t e) -> p t e", t=TILES))
                own(ts(rt[:, 10, 0], ps[:, 1, 2 * NE:3 * NE], float(P), None, ALU.is_gt))
                dve.sem_inc(count_read, 1)
                flat = route.rearrange("p q t e -> p (q t) e")
                own(copy(table[:, 1:1 + NE].rearrange("p e q t -> p e (q t)"), flat.rearrange("p q e -> p e q")))

            def second_passes():
                flat = route.rearrange("p q t e -> p (q t) e")
                own(nc.vector.tensor_tensor_scan(rt[:, 11, 0], rt[:, 10, 0], zero_r[:, 0:NE].bitcast(F32), 0.0,
                                                 ALU.add, ALU.add))
                own(ts(expert_f[:, MAX_OVER:MAX_OVER + 1], rt[:, 11, 0, NE - 1:NE], float(NE), None, ALU.add))
                for j in range(MAX_OVER):
                    own(stt(rt[:, 12 + j, 0], rt[:, 11, 0], float(j + 1), rt[:, 10, 0], ALU.is_equal, ALU.mult))
                    own(tt(rt[:, 12 + j, 1], rt[:, 12 + j, 0], index[:], ALU.mult))
                    own(reduce(expert_f[:, j:j + 1], rt[:, 12 + j, 1], AX.X, ALU.add))
                    own(tt(rt[:, 16:19].rearrange("p q t e -> p (q t) e"), flat,
                           rt[:, 12 + j, 0].unsqueeze(1).to_broadcast([P, 3 * TILES, NE]), ALU.mult))
                    own(reduce(table[:, 1 + NE + j].rearrange("p q t -> p (q t)"),
                               rt[:, 16:19].rearrange("p q t e -> p (q t) e"), AX.X, ALU.add))
                    own(ts(table[:, 1 + NE + j, 0], table[:, 1 + NE + j, 0], -float(P), None, ALU.add))
                own(copy(expert_i[:, 0:MAX_OVER + 1], expert_f[:, 0:MAX_OVER + 1]))
                dve.sem_inc(passes_ready, 1)

            dve.wait_ge(c_ready, 1)
            own(nc.vector.memset(zero_r[:].bitcast(F32), 0.0))
            for k in range(KC):
                dve.wait_ge(start_landed[k], 16)
                for part in range(2):
                    if k:
                        dve.wait_ge(start_used, 2 * (k - 1) + part + 1)
                    else:
                        dve.wait_ge(bias_landed, 16 * (part + 1))
                    stt(ada_sum[:, part], ada_start[:, k, part], c_silu[:, k:k + 1],
                        ada_sum[:, part] if k else ada_bias[:], ALU.mult, ALU.add).then_inc(start_used, 1)
                    if k == 0:
                        dve.wait_ge(start_used, part + 1)
                        dve.sem_inc(bias_used, 1)
            scale(0)
            norm(0)
            mixer(0)
            close(0)
            norm(1)
            ffn(FFN_AT[0], 0, 0, True)
            done[0] = FFN_AT[0] + PASS_UNITS
            split_to(MIX_AT[1] + 2)
            close(1)
            norm(2)
            mixer(1)
            close(2)
            norm(3)
            for k in range(AHEAD):
                split((FFN_AT[1] + k, 0, 0))
            dve.wait_ge(moeconst_ready, 1)
            dve.wait_ge(router_done, 1)
            routing()
            pick(0)
            second_passes()
            dve.wait_ge(xg_half, 1)
            gathered_low()
            gate(3)
            passes = dve.value_load(expert_i[0:1, MAX_OVER:MAX_OVER + 1], min_val=NE, max_val=NE + MAX_OVER)
            ffn(FFN_AT[1], 0, FB, False)
            with dve.Fori(1, passes) as pas:
                ffn(FFN_AT[1], pas, FB, False)
            gather_sum(passes)
            dve.wait_ge(summed, passes * 2)
            close(3)


_INS = ["x", "c", "w_ada", "b_ada", "norm_g", "w_in", "fox_f_bias", "diff_lambda", "diff_subln_g", "w_branch",
        "w_out", "ffn_w_gate", "ffn_w_up", "ffn_w_down", "moe_router", "moe_w_gate", "moe_w_up", "moe_w_down"]
_OUTS = [((1, SEQ, D), "float32")]


def kernel(**inputs):
    import numpy as _np
    import concourse.bacc as _bacc
    from concourse import mybir as _mybir
    from concourse.bass_utils import run_bass_kernel_spmd as _run

    nc = _bacc.Bacc("TRN2", target_bir_lowering=False, num_devices=1, dynamic_dma_scratch_size=1024)
    arrays, args = {}, []
    for name in _INS:
        a = _np.ascontiguousarray(inputs[name])
        arrays[f"in_{name}_dram"] = a
        args.append(nc.dram_tensor(f"in_{name}_dram", a.shape, _mybir.dt.from_np(a.dtype), kind="ExternalInput").ap())
    for i, (shape, dtype) in enumerate(_OUTS):
        dt = _mybir.dt.from_np(_np.dtype(dtype))
        args.append(nc.dram_tensor(f"out_{i}_dram", shape, dt, kind="ExternalOutput").ap())
    build(nc, *args)
    r = _run(nc, [arrays], core_ids=[0])
    return r.results[0]["out_0_dram"]
```
